# Optimizing a Trainium2 kernel written in Bass

```python
import jax, jax.numpy as jnp
from jax import lax
import numpy as np

D_MODEL = 1024
BATCH = 1
SEQ = 512
DEPTH = 2

MEM_LEN = 256
D_FF = ((8 * D_MODEL // 3 + 255) // 256) * 256
D_MIX = D_MODEL
W_A = 3 * D_MIX // 8
W_B = 3 * D_MIX // 8
W_C = D_MIX - W_A - W_B
RG_BLOCK = 64
RG_HEADS = W_A // RG_BLOCK
RG_CONV_K = 4
RG_C = 8.0
GLA_HEADS = 4
GLA_DV = W_B // GLA_HEADS
GLA_DK = GLA_DV // 2
GLA_RANK = 16
GLA_TAU = 16.0
GLA_CHUNK = 64
CONV_K = 31
CONV_GROUPS = 4
XA_HEADS = 4
XA_HEAD_DIM = D_MODEL // XA_HEADS
ALPHA = (2.0 * DEPTH) ** 0.25
BETA = (8.0 * DEPTH) ** -0.25
EPS = 1e-5
SPLIT_SIZES = (W_A, W_A, GLA_HEADS * GLA_DK, GLA_HEADS * GLA_DK, W_B, W_B, GLA_RANK, 2 * W_C)
N_IN_COLS = 2 * W_A + 2 * GLA_HEADS * GLA_DK + 2 * W_B + GLA_RANK + 2 * W_C

kernel_name = "hybrid_rglru_gla_conformer_deepnorm"

def layer_norm(x, g, b):
    xf = x.astype(jnp.float32)
    mu = jnp.mean(xf, axis=-1, keepdims=True)
    var = jnp.mean(jnp.square(xf - mu), axis=-1, keepdims=True)
    y = (xf - mu) * lax.rsqrt(var + EPS)
    return (y * g + b).astype(x.dtype)

def swiglu(x, w_in, w_out):
    gate, up = jnp.split(x @ w_in, 2, axis=-1)
    return (jax.nn.silu(gate) * up) @ w_out

def causal_dwconv(x, w, b):
    k, c = w.shape
    y = lax.conv_general_dilated(x, w[:, None, :].astype(x.dtype), window_strides=(1,),
                                 padding=[(k - 1, 0)],
                                 dimension_numbers=("NWC", "WIO", "NWC"),
                                 feature_group_count=c)
    return y + b

def split_cols(h):
    idx = []
    acc = 0
    for s in SPLIT_SIZES[:-1]:
        acc += s
        idx.append(acc)
    return jnp.split(h, idx, axis=-1)

def _lin_combine(left, right):
    a1, b1 = left
    a2, b2 = right
    return a1 * a2, a2 * b1 + b2

def rglru_group(xa, ya, conv_w, conv_b, w_r, b_r, w_i, b_i, lam):
    bsz, s, w = xa.shape
    xc = causal_dwconv(xa, conv_w, conv_b)
    xh = xc.reshape(bsz, s, RG_HEADS, RG_BLOCK)
    r = jax.nn.sigmoid(jnp.einsum("bshi,hij->bshj", xh, w_r).reshape(bsz, s, w) + b_r)
    i = jax.nn.sigmoid(jnp.einsum("bshi,hij->bshj", xh, w_i).reshape(bsz, s, w) + b_i)
    log_a = -RG_C * r.astype(jnp.float32) * jax.nn.softplus(-lam.astype(jnp.float32))
    a = jnp.exp(log_a)
    u = jnp.sqrt(-jnp.expm1(2.0 * log_a)) * (i * xc).astype(jnp.float32)
    _, h = lax.associative_scan(_lin_combine, (a, u), axis=1)
    return (h * jax.nn.gelu(ya.astype(jnp.float32))).astype(xa.dtype)

def gla_chunked(q, k, v, log_alpha):
    bsz, s, h, dk = q.shape
    dv = v.shape[-1]
    n = s // GLA_CHUNK
    q = (q * (dk ** -0.5)).reshape(bsz, n, GLA_CHUNK, h, dk)
    k = k.reshape(bsz, n, GLA_CHUNK, h, dk)
    v = v.reshape(bsz, n, GLA_CHUNK, h, dv)
    bcum = jnp.cumsum(log_alpha.reshape(bsz, n, GLA_CHUNK, h, dk), axis=2)
    b_last = bcum[:, :, -1:]
    q_dec = q * jnp.exp(bcum)
    k_inv = k * jnp.exp(-bcum)
    scores = jnp.einsum("bnihd,bnjhd->bnhij", q_dec, k_inv)
    causal = jnp.tril(jnp.ones((GLA_CHUNK, GLA_CHUNK), dtype=bool))
    scores = jnp.where(causal, scores, 0.0)
    o_intra = jnp.einsum("bnhij,bnjhe->bnihe", scores, v)
    k_tail = k * jnp.exp(b_last - bcum)
    u = jnp.einsum("bnchd,bnche->bnhde", k_tail, v)
    decay = jnp.exp(b_last[:, :, 0])

    def step(state, inp):
        dec, inc = inp
        return dec[..., None] * state + inc, state

    init = jnp.zeros((bsz, h, dk, dv), jnp.float32)
    _, s_prev = lax.scan(step, init, (jnp.moveaxis(decay, 1, 0), jnp.moveaxis(u, 1, 0)))
    s_prev = jnp.moveaxis(s_prev, 0, 1)
    o_inter = jnp.einsum("bnihd,bnhde->bnihe", q_dec, s_prev)
    return (o_intra + o_inter).reshape(bsz, s, h, dv)

def gla_group(q, k, v, g, lr, w_gate, b_gate, norm_g):
    bsz, s, _ = q.shape
    f32 = jnp.float32
    gate_pre = (lr @ w_gate + b_gate).astype(f32)
    log_alpha = (jax.nn.log_sigmoid(gate_pre) / GLA_TAU).reshape(bsz, s, GLA_HEADS, GLA_DK)
    o = gla_chunked(q.astype(f32).reshape(bsz, s, GLA_HEADS, GLA_DK),
                    k.astype(f32).reshape(bsz, s, GLA_HEADS, GLA_DK),
                    v.astype(f32).reshape(bsz, s, GLA_HEADS, GLA_DV), log_alpha)
    o = o * lax.rsqrt(jnp.mean(jnp.square(o), axis=-1, keepdims=True) + EPS) * norm_g
    o = o.reshape(bsz, s, W_B) * jax.nn.silu(g.astype(f32))
    return o.astype(q.dtype)

def conformer_conv_group(c, dw_w, dw_b, gn_g, gn_b):
    bsz, s, _ = c.shape
    a, gate = jnp.split(c, 2, axis=-1)
    u = causal_dwconv(a * jax.nn.sigmoid(gate), dw_w, dw_b)
    uf = u.astype(jnp.float32).reshape(bsz, s, CONV_GROUPS, W_C // CONV_GROUPS)
    mu = jnp.mean(uf, axis=-1, keepdims=True)
    var = jnp.mean(jnp.square(uf - mu), axis=-1, keepdims=True)
    un = ((uf - mu) * lax.rsqrt(var + EPS)).reshape(bsz, s, W_C) * gn_g + gn_b
    return jax.nn.silu(un).astype(c.dtype)

def hybrid_mixer(x, w_in, rg_conv_w, rg_conv_b, rg_w_r, rg_b_r, rg_w_i, rg_b_i, rg_lambda,
                 gla_w_gate, gla_b_gate, gla_norm_g, cv_dw_w, cv_dw_b, cv_gn_g, cv_gn_b, w_out):
    xa, ya, q, k, v, g, lr, c = split_cols(x @ w_in)
    out_a = rglru_group(xa, ya, rg_conv_w, rg_conv_b, rg_w_r, rg_b_r, rg_w_i, rg_b_i, rg_lambda)
    out_b = gla_group(q, k, v, g, lr, gla_w_gate, gla_b_gate, gla_norm_g)
    out_c = conformer_conv_group(c, cv_dw_w, cv_dw_b, cv_gn_g, cv_gn_b)
    return jnp.concatenate([out_a, out_b, out_c], axis=-1) @ w_out

def memory_cross_attn(x, mem, w_q, w_kv, w_o):
    bsz, s, _ = x.shape
    m = mem.shape[1]
    q = (x @ w_q).reshape(bsz, s, XA_HEADS, XA_HEAD_DIM)
    k, v = jnp.split(mem @ w_kv, 2, axis=-1)
    k = k.reshape(bsz, m, XA_HEADS, XA_HEAD_DIM)
    v = v.reshape(bsz, m, XA_HEADS, XA_HEAD_DIM)
    scores = jnp.einsum("bshd,bmhd->bhsm", q, k).astype(jnp.float32) * (XA_HEAD_DIM ** -0.5)
    p = jax.nn.softmax(scores, axis=-1).astype(x.dtype)
    o = jnp.einsum("bhsm,bmhd->bshd", p, v).reshape(bsz, s, D_MODEL)
    return o @ w_o

def setup_inputs(seed: int = 0) -> dict:
    key = jax.random.key(seed)
    ks = iter(jax.random.split(key, 64))

    def nrm(shape, scale):
        return jax.random.normal(next(ks), shape, jnp.float32) * scale

    def gain(shape):
        return 1.0 + nrm(shape, 0.02)

    L = DEPTH
    u = jax.random.uniform(next(ks), (L, W_A), jnp.float32, minval=0.9, maxval=0.999)
    s_a = u ** (1.0 / RG_C)
    rg_lambda = jnp.log(s_a) - jnp.log1p(-s_a)
    xa_w_kv = jnp.concatenate([nrm((L, D_MODEL, D_MODEL), D_MODEL ** -0.5),
                               nrm((L, D_MODEL, D_MODEL), BETA * D_MODEL ** -0.5)], axis=-1)
    return {
        "x": nrm((BATCH, SEQ, D_MODEL), 1.0),
        "mem": nrm((BATCH, MEM_LEN, D_MODEL), 1.0),
        "ffn1_w_in": nrm((L, D_MODEL, 2 * D_FF), D_MODEL ** -0.5),
        "ffn1_w_out": nrm((L, D_FF, D_MODEL), BETA * D_FF ** -0.5),
        "ln1_g": gain((L, D_MODEL)),
        "ln1_b": nrm((L, D_MODEL), 0.02),
        "mix_w_in": nrm((L, D_MODEL, N_IN_COLS), D_MODEL ** -0.5),
        "rg_conv_w": nrm((L, RG_CONV_K, W_A), RG_CONV_K ** -0.5),
        "rg_conv_b": nrm((L, W_A), 0.01),
        "rg_w_r": nrm((L, RG_HEADS, RG_BLOCK, RG_BLOCK), RG_BLOCK ** -0.5),
        "rg_b_r": nrm((L, W_A), 0.01),
        "rg_w_i": nrm((L, RG_HEADS, RG_BLOCK, RG_BLOCK), RG_BLOCK ** -0.5),
        "rg_b_i": nrm((L, W_A), 0.01),
        "rg_lambda": rg_lambda,
        "gla_w_gate": nrm((L, GLA_RANK, GLA_HEADS * GLA_DK), GLA_RANK ** -0.5),
        "gla_b_gate": nrm((L, GLA_HEADS * GLA_DK), 0.01),
        "gla_norm_g": gain((L, GLA_DV)),
        "cv_dw_w": nrm((L, CONV_K, W_C), CONV_K ** -0.5),
        "cv_dw_b": nrm((L, W_C), 0.01),
        "cv_gn_g": gain((L, W_C)),
        "cv_gn_b": nrm((L, W_C), 0.02),
        "mix_w_out": nrm((L, D_MIX, D_MODEL), BETA * D_MIX ** -0.5),
        "ln2_g": gain((L, D_MODEL)),
        "ln2_b": nrm((L, D_MODEL), 0.02),
        "xa_w_q": nrm((L, D_MODEL, D_MODEL), D_MODEL ** -0.5),
        "xa_w_kv": xa_w_kv,
        "xa_w_o": nrm((L, D_MODEL, D_MODEL), BETA * D_MODEL ** -0.5),
        "ln3_g": gain((L, D_MODEL)),
        "ln3_b": nrm((L, D_MODEL), 0.02),
        "ffn2_w_in": nrm((L, D_MODEL, 2 * D_FF), D_MODEL ** -0.5),
        "ffn2_w_out": nrm((L, D_FF, D_MODEL), BETA * D_FF ** -0.5),
        "ln4_g": gain((L, D_MODEL)),
        "ln4_b": nrm((L, D_MODEL), 0.02),
    }

def reference(x, mem, ffn1_w_in, ffn1_w_out, ln1_g, ln1_b, mix_w_in, rg_conv_w, rg_conv_b,
              rg_w_r, rg_b_r, rg_w_i, rg_b_i, rg_lambda, gla_w_gate, gla_b_gate, gla_norm_g,
              cv_dw_w, cv_dw_b, cv_gn_g, cv_gn_b, mix_w_out, ln2_g, ln2_b, xa_w_q, xa_w_kv,
              xa_w_o, ln3_g, ln3_b, ffn2_w_in, ffn2_w_out, ln4_g, ln4_b):
    for l in range(DEPTH):
        x = layer_norm(ALPHA * x + 0.5 * swiglu(x, ffn1_w_in[l], ffn1_w_out[l]), ln1_g[l], ln1_b[l])
        mix = hybrid_mixer(x, mix_w_in[l], rg_conv_w[l], rg_conv_b[l], rg_w_r[l], rg_b_r[l],
                           rg_w_i[l], rg_b_i[l], rg_lambda[l], gla_w_gate[l], gla_b_gate[l],
                           gla_norm_g[l], cv_dw_w[l], cv_dw_b[l], cv_gn_g[l], cv_gn_b[l],
                           mix_w_out[l])
        x = layer_norm(ALPHA * x + mix, ln2_g[l], ln2_b[l])
        x = layer_norm(ALPHA * x + memory_cross_attn(x, mem, xa_w_q[l], xa_w_kv[l], xa_w_o[l]),
                       ln3_g[l], ln3_b[l])
        x = layer_norm(ALPHA * x + 0.5 * swiglu(x, ffn2_w_in[l], ffn2_w_out[l]), ln4_g[l], ln4_b[l])
    return x


_drawn_inputs = setup_inputs


def setup_inputs(seed=0):
    import zlib

    import numpy as np

    out = dict(_drawn_inputs(seed))
    spreads = {}
    factors = {'rg_conv_b': 6.127,
     'rg_b_r': 8.0,
     'rg_b_i': 8.0,
     'gla_w_gate': 2.94,
     'gla_b_gate': 8.0,
     'gla_norm_g': 8.0,
     'cv_dw_b': 8.0,
     'cv_gn_g': 8.0,
     'cv_gn_b': 8.0}
    for name, (base, spread) in spreads.items():
        noise = np.random.default_rng([zlib.crc32(name.encode()), seed]).standard_normal(out[name].shape)
        drawn = base * np.exp(spread * noise) if base else spread * noise
        out[name] = __import__('jax').numpy.asarray(drawn.astype(out[name].dtype))
    for name, factor in factors.items():
        out[name] = (out[name] * factor).astype(out[name].dtype)
    return out
```

```python
import concourse.bass as bass
from concourse import mybir
from contextlib import ExitStack

F32 = mybir.dt.float32
F32R = mybir.dt.float32r
U32 = mybir.dt.uint32
ALU = mybir.AluOpType
ACT = mybir.ActivationFunctionType
AX = mybir.AxisListType

LAYERS = 2
SEQ = 512
D = 1024
MEM = 256
D_FF = 2816
P = 128
KT = D // P
FT = D_FF // P
TT = SEQ // P
ALPHA = (2.0 * LAYERS) ** 0.25
EPS = 1e-5

W_A, W_B, W_C = 384, 384, 256
AT, CT = W_A // P, W_C // P
RG_K, CONV_K = 4, 31
HEADS, DK, DV, RANK, CHUNK = 4, 48, 96, 16, 64
NCHUNK = SEQ // CHUNK
LR_ROW = DV
MIXK = AT + HEADS + CT
XH, XD = 4, 256
XSCALE = XD ** -0.5

UNITS = 12
RAW, SPLIT = 4, 2
S_IN = (0, 120)
S_OUT = (44, 164)
S_MIX, S_MIXOUT, S_KV, S_Q, S_AO = 60, 80, 88, 104, 112
SLOTS = 180
V_SLOT = 13


def slot_width(s):
    if S_OUT[0] <= s < S_MIX or s >= S_OUT[1]:
        return FT // 2 * P
    if S_MIX + V_SLOT <= s < S_MIX + V_SLOT + 2:
        return 4 * W_B
    if S_MIXOUT <= s < S_KV:
        return MIXK * P
    return KT * P


V_LN = 0
V_CW = 64
V_CB = V_CW + RG_K * AT
V_BR = V_CB + AT
V_BI = V_BR + AT
V_LAM = V_BI + AT
V_BG = V_LAM + AT
V_NG = V_BG + 2
V_DW = V_NG + 1
V_DB = V_DW + CONV_K * CT
V_GG = V_DB + CT
V_GB = V_GG + CT
NV = V_GB + CT

C_ID, C_ONE, C_B64, C_O96, C_MASK, C_START, C_AVG = 0, 128, 256, 384, 512, 640, 1152
NC_ = 1153

MIX_TILES = [("xa", 0, 0, 0), ("xa", 1, 0, 0), ("xa", 2, 0, 0), ("cg", 0, 0, 0), ("cg", 1, 1, 0),
             ("ca", 0, 2, 0), ("ca", 1, 3, 0), ("k", 0, 4, 0), ("k", 1, 5, 0), ("q", 0, 0, 1),
             ("q", 1, 0, 2), ("g", 0, 6, 0), ("g", 1, 7, 0), ("g", 2, 8, 0), ("g", 3, 9, 0),
             ("ya", 0, 10, 0), ("ya", 1, 11, 0), ("ya", 2, 16, 0)]
MIX_SLOT = {(k, i): n if n < 13 else n + 2 for n, (k, i, _, _) in enumerate(MIX_TILES)}
EVAC = ([("xa", 0), ("xa", 1), ("xa", 2), ("cg", 0), ("cg", 1), ("k", 0), ("k", 1), ("q", 0),
         ("q", 1), ("g", 0), ("g", 1)] + [("v", t) for t in range(4)] +
        [("g", 2), ("g", 3), ("ya", 0), ("ya", 1), ("ya", 2)])
EVACS = len(EVAC)
EV = {e: n + 1 for n, e in enumerate(EVAC)}


def hybrid_decoder(nc, x_in, mem_in, consts_in, vecs_in, mats_in, w_in1, w_out1, w_in2, w_out2,
                   w_mix, w_v, w_mixout, w_kv, w_q, w_o, out):
    ctx = ExitStack()
    with ctx:
        def sb(name, shape, dt=F32):
            return ctx.enter_context(nc.sbuf_tensor(name, shape, dt))

        def sem(name):
            return ctx.enter_context(nc.semaphore(name))

        x = sb("x", [P, KT, SEQ])
        act_hi = sb("act_hi", [P, MIXK, SEQ], F32R)
        act_lo = sb("act_lo", [P, MIXK, SEQ], F32R)
        raw = sb("raw", [P, RAW, UNITS * P])
        w_hi = sb("w_hi", [P, SPLIT, UNITS * P], F32R)
        w_lo = sb("w_lo", [P, SPLIT, UNITS * P], F32R)
        work = sb("work", [P, 4, SEQ])
        consts = sb("consts", [P, NC_])
        vecs = sb("vecs", [P, NV])
        mats = sb("mats", [P, 1024])
        small = sb("small", [P, 48])
        lam = sb("lam", [P, 13 * AT])

        with ExitStack() as part:
            h_hi = part.enter_context(nc.sbuf_tensor("h_hi", [P, FT, SEQ], F32R))
            h_lo = part.enter_context(nc.sbuf_tensor("h_lo", [P, FT, SEQ], F32R))
        with ExitStack() as part:
            tmp = part.enter_context(nc.sbuf_tensor("tmp", [P, 2 * FT * SEQ], F32))
        with ExitStack() as part:
            kT_hi = part.enter_context(nc.sbuf_tensor("kT_hi", [P, KT, MEM], F32R))
            kT_lo = part.enter_context(nc.sbuf_tensor("kT_lo", [P, KT, MEM], F32R))
            v_hi = part.enter_context(nc.sbuf_tensor("v_hi", [P, 2, D], F32R))
            v_lo = part.enter_context(nc.sbuf_tensor("v_lo", [P, 2, D], F32R))
            with ExitStack() as inner:
                mem_raw = inner.enter_context(nc.sbuf_tensor("mem_raw", [P, KT, MEM], F32))
                mem_hi = inner.enter_context(nc.sbuf_tensor("mem_hi", [P, KT, MEM], F32R))
                mem_lo = inner.enter_context(nc.sbuf_tensor("mem_lo", [P, KT, MEM], F32R))
                with ExitStack() as last:
                    k_st = last.enter_context(nc.sbuf_tensor("k_st", [P, KT, MEM], F32))
                    v_st = last.enter_context(nc.sbuf_tensor("v_st", [P, 2, D], F32))
                q_hi = inner.enter_context(nc.sbuf_tensor("q_hi", [P, KT, SEQ], F32R))
                q_lo = inner.enter_context(nc.sbuf_tensor("q_lo", [P, KT, SEQ], F32R))
            with ExitStack() as inner:
                probs = inner.enter_context(nc.sbuf_tensor("probs", [P, 2, TT, MEM], F32))
                pT_hi = inner.enter_context(nc.sbuf_tensor("pT_hi", [P, 2, SEQ], F32R))
                pT_lo = inner.enter_context(nc.sbuf_tensor("pT_lo", [P, 2, SEQ], F32R))
        region_end = ctx.enter_context(nc.sbuf_tensor("region", [P, 2 * FT * SEQ], F32))

        psum = ctx.enter_context(nc.psum_tensor("psum", [P, 8, SEQ], F32))

        ident = consts[:, C_ID:C_ID + P]
        ones = consts[:, C_ONE:C_ONE + P]
        block64 = consts[:, C_B64:C_B64 + P]
        ones96 = consts[0:DV, C_O96:C_O96 + DV]
        score_mask = consts[:, C_MASK:C_MASK + P].bitcast(U32)
        not_start = consts[:, C_START:C_START + SEQ]
        average = consts[:, C_AVG:C_AVG + 1]

        zsum, zsqsum = work[:, 0, :], work[:, 1, :]

        def zsq(m):
            return work[:, 2 + m % 2, :]

        diag = work[:, 2:4, :].rearrange("p a (t c) -> p (a t) c", c=P)

        def tile(n):
            return tmp[:, n * SEQ:(n + 1) * SEQ]

        XA_W, U_W = SEQ + RG_K - 1, SEQ + CONV_K - 1
        xa_pad = tmp[:, 0:AT * XA_W].rearrange("p (t s) -> p t s", t=AT)
        u_pad = tmp[:, AT * XA_W:AT * XA_W + CT * U_W].rearrange("p (t s) -> p t s", t=CT)
        XC = [tile(6 + t) for t in range(AT)]
        RR = [tile(9 + t) for t in range(AT)]
        II = [tile(12 + t) for t in range(AT)]
        EE = [tile(15 + t) for t in range(AT)]
        TH = [xa_pad[:, t, 0:SEQ] for t in range(AT)]
        CC = [tile(18 + t) for t in range(CT)]
        SQ = [u_pad[:, t, 0:SEQ] for t in range(CT)]
        KK = [tile(20 + t) for t in range(2)]
        QQ = [tile(22 + t) for t in range(2)]
        GP = [tile(24 + t) for t in range(2)]
        CU = [tile(26 + t) for t in range(2)]
        EB = [tile(28 + t) for t in range(2)]
        KI = [tile(30 + t) for t in range(2)]
        v_tok = tmp[:, 32 * SEQ:35 * SEQ].rearrange("p (t e) -> p t e", t=TT)
        k_tok = tmp[:, 35 * SEQ:37 * SEQ].rearrange("p (t e) -> p t e", t=TT)
        SC = [tile(37 + t) for t in range(2)]
        lr = tile(37)[LR_ROW:LR_ROW + RANK, :]
        state = tmp[:, 39 * SEQ:42 * SEQ].rearrange("p (n g e) -> p n g e", n=NCHUNK, g=2)
        GG = [tile(42), tile(43), tile(20), tile(21)]
        YA = EE
        OO = [tile(9), tile(10), tile(11), tile(12)]
        OSQ = CU
        RS = [tile(13), tile(14)]

        consts_loaded, x_loaded = sem("consts_loaded"), sem("x_loaded")
        vectors_loaded, mem_loaded = sem("vectors_loaded"), sem("mem_loaded")
        raw_loaded = [sem(f"raw_loaded{j}") for j in range(RAW)]
        w_hi_made = sem("w_hi_made")
        slot_split = sem("slot_split")
        slot_multiplied = sem("slot_multiplied")
        eps_set = sem("eps_set")
        x_hi_made = sem("x_hi_made")
        x_split = sem("x_split")
        gate_silu = sem("gate_silu")
        h_made = sem("h_made")
        h_split = sem("h_split")
        z_added = sem("z_added")
        z_squared = sem("z_squared")
        z_summed = sem("z_summed")
        stats_ready = sem("stats_ready")
        var_ready = sem("var_ready")
        std_ready = sem("std_ready")
        diag_ready = sem("diag_ready")
        bcast_ready = sem("bcast_ready")
        y_centered = sem("y_centered")
        evac = sem("evac")
        ca_used = sem("ca_used")
        lam_log, lam_q, lam_tanh, lam_ready = (sem("lam_log"), sem("lam_q"), sem("lam_tanh"),
                                               sem("lam_ready"))
        xc_ready = sem("xc_ready")
        rg_gate_ready = sem("rg_gate_ready")
        rg_gate_read = sem("rg_gate_read")
        rg_factors = sem("rg_factors")
        rg_scanned = sem("rg_scanned")
        gla_gate_ready = sem("gla_gate_ready")
        gla_gate_read = sem("gla_gate_read")
        gla_log = sem("gla_log")
        gla_cum = sem("gla_cum")
        gla_exp = sem("gla_exp")
        gla_qk = sem("gla_qk")
        ktok_ready, ktok_read = sem("ktok_ready"), sem("ktok_read")
        u_ready, state_ready = sem("u_ready"), sem("state_ready")
        score_ready, score_masked = sem("score_ready"), sem("score_masked")
        o_ready, o_read = sem("o_ready"), sem("o_read")
        rms_ready, rms_root = sem("rms_ready"), sem("rms_root")
        conv_done = sem("conv_done")
        gn_mean, gn_centered, gn_squared = sem("gn_mean"), sem("gn_centered"), sem("gn_squared")
        gn_var, gn_root, gn_scaled = sem("gn_var"), sem("gn_root"), sem("gn_scaled")
        mixed = sem("mixed")
        mixed_hi, mixed_split = sem("mixed_hi"), sem("mixed_split")
        mem_hi_made, mem_split = sem("mem_hi_made"), sem("mem_split")
        kv_read = sem("kv_read")
        kv_split = sem("kv_split")
        q_hi_made, q_split = sem("q_hi_made"), sem("q_split")
        qk_ready = sem("qk_ready")
        max_ready = sem("max_ready")
        exp_ready = sem("exp_ready")
        probs_ready = sem("probs_ready")
        pT_ready, pT_hi_made, pT_split = sem("pT_ready"), sem("pT_hi_made"), sem("pT_split")
        ctx_ready, ctx_hi_made, ctx_split = sem("ctx_ready"), sem("ctx_hi_made"), sem("ctx_split")
        out_stored = sem("out_stored")
        pool_wait_carrier, dve_wait_carrier = sem("pool_wait_carrier"), sem("dve_wait_carrier")

        def bank(b, rows=P, cols=SEQ):
            return psum[0:rows, b, 0:cols]

        block = ctx.enter_context(nc.Block())

        @block.sync
        def _(sp):
            sp.dma_start(consts[:, :], consts_in).then_inc(consts_loaded, 16)
            sp.dma_start(x[:, :, :], x_in).then_inc(x_loaded, 16)

            def load(dram, layer, s, i, j, per_layer, width):
                sp.wait_ge(slot_split, layer * SLOTS + s + 1)
                src = dram[bass.ds(layer * per_layer + i, 1)].rearrange("a p n -> (a p) n")
                sp.dma_start(raw[:, j, 0:width], src).then_inc(raw_loaded[j], 16)

            def stage(dram, layer, s0, n, width):
                with sp.Fori(0, n // RAW) as it:
                    for j in range(RAW):
                        load(dram, layer, it * RAW + (s0 + j), it * RAW + j, j, n, width)

            with sp.Fori(0, LAYERS) as layer:
                stage(w_in1, layer, S_IN[0], 44, 8 * P)
                stage(w_out1, layer, S_OUT[0], 16, 11 * P)
                for s in range(20):
                    if V_SLOT <= s < V_SLOT + 2:
                        load(w_v, layer, S_MIX + s, s - V_SLOT, s % RAW, 2, 12 * P)
                    else:
                        i = s if s < V_SLOT else s - 2
                        load(w_mix, layer, S_MIX + s, i, s % RAW, 18, 8 * P)
                stage(w_mixout, layer, S_MIXOUT, 8, MIXK * P)
                stage(w_kv, layer, S_KV, 16, 8 * P)
                stage(w_q, layer, S_Q, 8, 8 * P)
                stage(w_o, layer, S_AO, 8, 8 * P)
                stage(w_in2, layer, S_IN[1], 44, 8 * P)
                stage(w_out2, layer, S_OUT[1], 16, 11 * P)
            for part in range(4):
                sp.wait_ge(x_hi_made, KT + LAYERS * 4 * KT - KT + 2 * (part + 1))
                sp.dma_start(out[:, 2 * part:2 * part + 2, :],
                             x[:, 2 * part:2 * part + 2, :]).then_inc(out_stored, 16)
            sp.wait_ge(out_stored, 64)

        @block.gpsimd
        def _(pool):
            pool.sem_inc(slot_split, RAW)

            def split(layer, s, j, width):
                pool.wait_ge(w_hi_made, layer * (SLOTS - 2) + s - 1)
                r = j % SPLIT
                nc.gpsimd.tensor_tensor(w_lo[:, r, 0:width], raw[:, j, 0:width],
                                        w_hi[:, r, 0:width].bitcast(F32),
                                        ALU.subtract).then_inc(slot_split, 1)

            def split_first(layer, s):
                pool.wait_ge(raw_loaded[s], (layer * (SLOTS // RAW) + 1) * 16)
                pool.wait_ge(slot_multiplied, layer * SLOTS + s + 1)
                pool.sem_inc(pool_wait_carrier, 1)
                src = raw[:, s, 0:KT * P]
                nc.gpsimd.tensor_copy(w_hi[:, s, 0:KT * P], src)
                pool.drain()
                nc.gpsimd.tensor_tensor(w_lo[:, s, 0:KT * P], src,
                                        w_hi[:, s, 0:KT * P].bitcast(F32),
                                        ALU.subtract).then_inc(slot_split, 1)

            def rest(layer, s0, n, first):
                with pool.Fori(first, n // RAW) as it:
                    for j in range(RAW):
                        split(layer, it * RAW + (s0 + j), j, slot_width(s0))

            def split_x(layer, c):
                for k in range(KT):
                    pool.wait_ge(x_hi_made, layer * 4 * KT + c * KT + k + 1)
                    nc.gpsimd.tensor_tensor(act_lo[:, k, :], x[:, k, :],
                                            act_hi[:, k, :].bitcast(F32),
                                            ALU.subtract).then_inc(x_split, 1)

            def ffn(layer, f, c):
                s0 = S_IN[f]
                for j in range(RAW):
                    if j == SPLIT:
                        split_x(layer, c)
                    if f == 0 and j < SPLIT:
                        split_first(layer, j)
                    else:
                        split(layer, s0 + j, j, slot_width(s0))
                rest(layer, s0, 44, 1)
                rest(layer, S_OUT[f], 16, 0)

            with pool.Fori(0, LAYERS) as layer:
                ffn(layer, 0, 0)
                for s in range(20):
                    if s == SPLIT:
                        split_x(layer, 1)
                    split(layer, S_MIX + s, s % RAW, slot_width(S_MIX + s))
                for s in range(8):
                    if s == SPLIT:
                        for k in range(MIXK):
                            pool.wait_ge(mixed_hi, layer * MIXK + k + 1)
                            rows = DV if AT <= k < AT + HEADS else P
                            src = XC[k] if k < AT else OO[k - AT] if k < AT + HEADS else \
                                CC[k - AT - HEADS]
                            nc.gpsimd.tensor_tensor(act_lo[0:rows, k, :], src[0:rows, :],
                                                    act_hi[0:rows, k, :].bitcast(F32),
                                                    ALU.subtract).then_inc(mixed_split, 1)
                    split(layer, S_MIXOUT + s, s % RAW, slot_width(S_MIXOUT))
                for s in range(8):
                    if s == 6:
                        split_x(layer, 2)
                    split(layer, S_KV + s, s % RAW, slot_width(S_KV))
                rest(layer, S_KV, 16, 2)
                rest(layer, S_Q, 8, 0)
                rest(layer, S_AO, 8, 0)
                ffn(layer, 1, 3)

        @block.tensor
        def _(pe):
            pe.sem_inc(slot_multiplied, SPLIT)
            pe.wait_ge(consts_loaded, 16)

            def passes(o, a_hi, a_lo, b_hi, b_lo, start, stop):
                nc.tensor.matmul(o, a_hi, b_hi, start=start, stop=False)
                nc.tensor.matmul(o, a_hi, b_lo, start=False, stop=False)
                return nc.tensor.matmul(o, a_lo, b_hi, start=False, stop=stop)

            def weight(r, u, rows=P):
                return (w_hi[0:rows, r, u * P:(u + 1) * P], w_lo[0:rows, r, u * P:(u + 1) * P])

            def act(k, rows=P):
                return act_hi[0:rows, k, :], act_lo[0:rows, k, :]

            def slot_ready(layer, s):
                pe.wait_ge(slot_split, layer * SLOTS + s + (RAW + 1))

            def tile_of(o, r, operand, n):
                for k in range(n):
                    last = passes(o, *weight(r, k), *operand(k), k == 0, k == n - 1)
                last.then_inc(slot_multiplied, 1)

            def first_pair(layer, s, n, rows, arrived):
                slot_ready(layer, s)
                slot_ready(layer, s + 1)
                for k in range(n):
                    arrived(k)
                    for j in range(2):
                        last = passes(bank(j), *weight(j, k, rows(k)), *act(k, rows(k)),
                                      k == 0, k == n - 1)
                        if k == n - 1:
                            last.then_inc(slot_multiplied, 1)

            def x_arrived(layer, c):
                return lambda k: pe.wait_ge(x_split, layer * 4 * KT + c * KT + k + 1)

            def stats(layer, n):
                pe.wait_ge(z_summed, layer * 4 * KT + (n + 1) * KT + 2)
                for a in range(2):
                    for t in range(TT):
                        last = nc.tensor.matmul(psum[:, 6, a * TT + t:a * TT + t + 1],
                                                work[:, a, t * P:(t + 1) * P], average,
                                                start=True, stop=True)
                last.then_inc(stats_ready, 1)

            def bcast(layer, n):
                pe.wait_ge(diag_ready, layer * 4 + n + 1)
                for a in range(2):
                    for t in range(TT):
                        last = nc.tensor.matmul(psum[:, 4 + a, t * P:(t + 1) * P], ones,
                                                diag[:, a * TT + t, :], start=True, stop=True)
                last.then_inc(bcast_ready, 1)

            def ffn(layer, f, c, n):
                base = layer * (2 * FT) + f * FT

                def pair(i, j, p0, first):
                    s = p0
                    pe.wait_ge(gate_silu, base + i + 1)
                    pe.wait_ge(h_made, base + i + 1)
                    if first:
                        first_pair(layer, s, KT, lambda k: P, x_arrived(layer, c))
                        return
                    for g in range(2):
                        slot_ready(layer, s + g)
                        tile_of(bank(2 * j + g), g, act, KT)

                pair(0, 0, S_IN[f], True)
                pair(1, 1, S_IN[f] + 2, False)
                with pe.Fori(1, FT // 2) as it:
                    for j in range(2):
                        pair(it * 2 + j, j, it * 4 + (S_IN[f] + 2 * j), False)
                with pe.Fori(0, KT // 2) as it:
                    pe.wait_ge(h_split, base + FT)
                    for j in range(2):
                        pe.wait_ge(z_added, layer * 4 * KT + it * 2 + (n * KT + j + 1))
                        for r in range(2):
                            slot_ready(layer, it * 4 + (S_OUT[f] + 2 * j + r))
                            for u in range(11):
                                k = 11 * r + u
                                last = passes(bank(j), *weight(r, u), h_hi[:, k, :], h_lo[:, k, :],
                                              k == 0, k == FT - 1)
                            last.then_inc(slot_multiplied, 1)
                stats(layer, n)
                bcast(layer, n)

            def out_rest(layer, s0, n, units, rows, first):
                with pe.Fori(first, KT // 2) as it:
                    if n == 2:
                        pe.wait_ge(ctx_split, layer * KT + KT)
                    for j in range(2):
                        pe.wait_ge(z_added, layer * 4 * KT + it * 2 + (n * KT + j + 1))
                        slot_ready(layer, it * 2 + (s0 + j))
                        for k in range(units):
                            last = passes(bank(j), *weight(j, k, rows(k)), *act(k, rows(k)),
                                          k == 0, k == units - 1)
                        last.then_inc(slot_multiplied, 1)

            def mixer(layer):
                E = layer * EVACS

                def project(kind, i):
                    n = [t[0:2] for t in MIX_TILES].index((kind, i))
                    _, _, by_act, by_dve = MIX_TILES[n]
                    if by_act:
                        pe.wait_ge(evac, E + by_act)
                    if by_dve:
                        pe.wait_ge(ca_used, layer * CT + by_dve)
                    s = S_MIX + MIX_SLOT[kind, i]
                    slot_ready(layer, s)
                    tile_of(bank(n % 4), s % SPLIT, act, KT)

                first_pair(layer, S_MIX, KT, lambda k: P, x_arrived(layer, 1))
                project("xa", 2)
                for i in range(2):
                    project("cg", i)
                for i in range(2):
                    project("ca", i)
                pe.wait_ge(vectors_loaded, layer * 32 + 32)
                for t in range(AT):
                    pe.wait_ge(xc_ready, layer * AT + t + 1)
                    for g in range(2):
                        n = 2 * t + g
                        if n >= 4:
                            pe.wait_ge(rg_gate_read, layer * 6 + n - 3)
                        nc.tensor.matmul(bank(4 + n % 4), mats[:, (AT * g + t) * P:][:, 0:P],
                                         XC[t], start=True, stop=True).then_inc(rg_gate_ready, 1)
                for kind, i in (("k", 0), ("k", 1), ("q", 0), ("q", 1), ("g", 0), ("g", 1)):
                    project(kind, i)
                pe.wait_ge(evac, E + EV["g", 0])
                pe.wait_ge(rg_gate_read, layer * 6 + 6)
                for g in range(2):
                    last = nc.tensor.matmul(bank(6 + g),
                                            mats[LR_ROW:LR_ROW + RANK, (2 * AT + g) * P:][:, 0:P],
                                            lr, start=True, stop=True)
                last.then_inc(gla_gate_ready, 1)
                pe.wait_ge(gla_gate_read, layer + 1)
                for s in range(2):
                    slot_ready(layer, S_MIX + V_SLOT + s)
                    r = (V_SLOT + s) % SPLIT
                    for u in range(4):
                        k = 4 * s + u
                        for t in range(TT):
                            cols = slice(t * P, (t + 1) * P)
                            last = passes(bank(4 + t, P, W_B),
                                          act_hi[:, k, cols], act_lo[:, k, cols],
                                          w_hi[:, r, u * W_B:(u + 1) * W_B],
                                          w_lo[:, r, u * W_B:(u + 1) * W_B],
                                          k == 0, k == KT - 1)
                    last.then_inc(slot_multiplied, 1)
                pe.wait_ge(evac, E + EV["v", 3])
                pe.wait_ge(gla_qk, layer * 2 + 2)
                for t in range(TT):
                    for g in range(2):
                        last = nc.tensor.transpose(
                            psum[:, 6 + t // 2, (t % 2 * 2 + g) * P:(t % 2 * 2 + g + 1) * P],
                            GP[g][:, t * P:(t + 1) * P], ident)
                last.then_inc(ktok_ready, 1)
                project("g", 2)
                pe.wait_ge(ktok_read, layer + 1)
                for n in range(NCHUNK - 1):
                    if n >= 2:
                        pe.wait_ge(state_ready, layer * (NCHUNK - 1) + n - 1)
                    t, r0 = n // 2, n % 2 * CHUNK
                    for g in range(2):
                        last = nc.tensor.matmul(
                            psum[:, 4 + n % 2, g * 2 * DV:(g + 1) * 2 * DV],
                            k_tok[r0:r0 + CHUNK, t, g * P:(g + 1) * P],
                            v_tok[r0:r0 + CHUNK, t, g * 2 * DV:(g + 1) * 2 * DV],
                            start=True, stop=True)
                    last.then_inc(u_ready, 1)
                project("g", 3)

                def scores(h):
                    if h < 2:
                        pe.wait_ge(state_ready, layer * (NCHUNK - 1) + NCHUNK - 1)
                    else:
                        pe.wait_ge(score_masked, layer * HEADS + h - 1)
                    g, r0 = h // 2, h % 2 * CHUNK
                    for t in range(TT):
                        cols = slice(t * P, (t + 1) * P)
                        last = nc.tensor.matmul(psum[:, 4 + h % 2, cols], KI[g][r0:r0 + CHUNK, cols],
                                                QQ[g][r0:r0 + CHUNK, cols], start=True, stop=True)
                    last.then_inc(score_ready, 1)

                def output(h):
                    pe.wait_ge(score_masked, layer * HEADS + h + 1)
                    if h >= 2:
                        pe.wait_ge(o_read, layer * HEADS + h - 1)
                    g, r0 = h // 2, h % 2 * CHUNK
                    for t in range(TT):
                        nc.tensor.matmul(psum[0:DV, 6 + h % 2, t * P:(t + 1) * P],
                                         v_tok[:, t, h * DV:(h + 1) * DV],
                                         SC[h % 2][:, t * P:(t + 1) * P], start=True, stop=False)
                        for n in (2 * t, 2 * t + 1):
                            if n:
                                cols = slice(n * CHUNK, (n + 1) * CHUNK)
                                last = nc.tensor.matmul(psum[0:DV, 6 + h % 2, cols],
                                                        state[r0:r0 + CHUNK, n, g, :],
                                                        QQ[g][r0:r0 + CHUNK, cols],
                                                        start=False, stop=n % 2 == 1)
                    last.then_inc(o_ready, 1)

                scores(0)
                scores(1)
                project("ya", 0)
                output(0)
                scores(2)
                output(1)
                project("ya", 1)
                scores(3)
                output(2)
                output(3)
                project("ya", 2)

                def rms(h):
                    pe.wait_ge(o_read, layer * HEADS + h + 1)
                    if h < 2:
                        pe.wait_ge(evac, E + EV["ya", 1 + h])
                    else:
                        pe.wait_ge(rms_root, layer * HEADS + h - 1)
                    nc.tensor.matmul(bank(h % 2, DV), ones96, OSQ[h % 2][0:DV, :],
                                     start=True, stop=True).then_inc(rms_ready, 1)

                rms(0)
                rms(1)
                for t in range(CT):
                    pe.wait_ge(conv_done, layer * CT + t + 1)
                    nc.tensor.matmul(bank(2 + t), block64, CC[t],
                                     start=True, stop=True).then_inc(gn_mean, 1)
                rms(2)
                rms(3)
                for t in range(CT):
                    pe.wait_ge(gn_squared, layer * CT + t + 1)
                    nc.tensor.matmul(bank(2 + t), block64, SQ[t],
                                     start=True, stop=True).then_inc(gn_var, 1)

                def rows(k):
                    return DV if AT <= k < AT + HEADS else P

                pe.wait_ge(rms_root, layer * HEADS + HEADS)
                first_pair(layer, S_MIXOUT, MIXK, rows,
                           lambda k: pe.wait_ge(mixed_split, layer * MIXK + k + 1))
                out_rest(layer, S_MIXOUT, 1, MIXK, rows, 1)

            def attention(layer):
                pe.wait_ge(mem_split, layer + 1)

                def k_tile(m):
                    if m < 2:
                        pe.wait_ge(gn_root, layer * CT + m + 1)
                    else:
                        pe.wait_ge(kv_read, layer * 12 + m - 1)
                    slot_ready(layer, S_KV + m)
                    tile_of(bank(2 + m % 2, P, MEM), m % SPLIT,
                            lambda k: (mem_hi[:, k, :], mem_lo[:, k, :]), KT)

                k_tile(0)
                k_tile(1)
                stats(layer, 1)
                k_tile(2)
                bcast(layer, 1)
                for m in range(3, KT):
                    k_tile(m)
                for half in range(2):
                    pe.wait_ge(kv_read, layer * 12 + 8 + 2 * half)
                    for s in range(4):
                        slot_ready(layer, S_KV + 8 + 4 * half + s)
                        for u in range(2):
                            k = 2 * s + u
                            for m in range(2):
                                last = passes(bank(2 + m), mem_hi[:, k, m * P:(m + 1) * P],
                                              mem_lo[:, k, m * P:(m + 1) * P],
                                              w_hi[:, s % SPLIT, u * SEQ:(u + 1) * SEQ],
                                              w_lo[:, s % SPLIT, u * SEQ:(u + 1) * SEQ],
                                              k == 0, k == KT - 1)
                        last.then_inc(slot_multiplied, 1)
                pe.wait_ge(x_split, layer * 4 * KT + 3 * KT)
                for m in range(KT):
                    pe.wait_ge(q_split, layer * KT + m + 1)
                    if m == 2:
                        pe.wait_ge(kv_read, layer * 12 + 12)
                    slot_ready(layer, S_Q + m)
                    tile_of(bank(m % 4), m % SPLIT, act, KT)

                def scores(h):
                    if h == 0:
                        pe.wait_ge(kv_split, layer * 2 + 1)
                        pe.wait_ge(q_split, layer * KT + KT + 4)
                    if h >= 2:
                        pe.wait_ge(exp_ready, layer * XH + h - 1)
                    for t in range(TT):
                        o = psum[:, h % 2 * 2 + t // 2, t % 2 * MEM:(t % 2 + 1) * MEM]
                        cols = slice(t * P, (t + 1) * P)
                        for u in range(2):
                            k = 2 * h + u
                            last = passes(o, q_hi[:, k, cols], q_lo[:, k, cols],
                                          kT_hi[:, k, :], kT_lo[:, k, :], u == 0, u == 1)
                    last.then_inc(qk_ready, 1)

                def context(h):
                    pe.wait_ge(probs_ready, layer * XH + h + 1)
                    if h >= 1:
                        pe.wait_ge(pT_split, layer * XH + h)
                    for t in range(TT):
                        for m in range(2):
                            last = nc.tensor.transpose(psum[:, 4 + m, t * P:(t + 1) * P],
                                                       probs[:, h % 2, t, m * P:(m + 1) * P], ident)
                    last.then_inc(pT_ready, 1)
                    pe.wait_ge(pT_split, layer * XH + h + 1)
                    if h == 0:
                        pe.wait_ge(kv_split, layer * 2 + 2)
                    for e in range(2):
                        if h >= 1:
                            pe.wait_ge(ctx_split, layer * KT + 2 * h - 1 + e)
                        cols = slice((2 * h + e) * P, (2 * h + e + 1) * P)
                        for m in range(2):
                            last = passes(bank(6 + e), v_hi[:, m, cols], v_lo[:, m, cols],
                                          pT_hi[:, m, :], pT_lo[:, m, :], m == 0, m == 1)
                        last.then_inc(ctx_ready, 1)

                scores(0)
                for h in range(XH):
                    if h + 1 < XH:
                        scores(h + 1)
                    context(h)
                out_rest(layer, S_AO, 2, KT, lambda k: P, 0)
                stats(layer, 2)
                bcast(layer, 2)

            with pe.Fori(0, LAYERS) as layer:
                ffn(layer, 0, 0, 0)
                mixer(layer)
                attention(layer)
                ffn(layer, 1, 3, 3)

        @block.scalar
        def _(act):
            act.sem_inc(gate_silu, 2)
            A = nc.scalar.activation

            def vec(c, rows=P):
                return vecs[0:rows, c:c + 1]

            act.wait_ge(eps_set, 1)
            A(small[:, 46:47], small[:, 47:48], ACT.Silu)
            act.wait_ge(x_loaded, 16)
            for k in range(KT):
                A(act_hi[:, k, :], x[:, k, :], ACT.Copy).then_inc(x_hi_made, 1)

            def advance(layer, s, place, rnd, width):
                act.wait_ge(slot_multiplied, layer * SLOTS + s + (SPLIT + 1))
                if width:
                    act.wait_ge(raw_loaded[place], (layer * (SLOTS // RAW) + rnd + 1) * 16)
                    A(w_hi[:, place % SPLIT, 0:width], raw[:, place, 0:width],
                      ACT.Copy).then_inc(w_hi_made, 1)

            def step(layer, s):
                n = s + SPLIT
                advance(layer, s, n % RAW, n // RAW, slot_width(n) if n < SLOTS else 0)

            def rounds(layer, s0, n, body):
                def adv(it, last):
                    def f(j):
                        m = j + SPLIT
                        if last:
                            step(layer, s0 + it * RAW + j)
                        else:
                            advance(layer, it * RAW + (s0 + j), m % RAW,
                                    it + (s0 // RAW + m // RAW), slot_width(s0))
                    return f
                with act.Fori(0, n // RAW - 1) as it:
                    body(it, adv(it, False))
                body(n // RAW - 1, adv(n // RAW - 1, True))

            def squares(layer, n, s0, per_tile):
                A(small[:, 46:47], small[:, 47:48], ACT.Sqrt)

                def body(it, adv):
                    for j in range(RAW // per_tile):
                        for r in range(per_tile):
                            adv(j * per_tile + r)
                        m = it * (RAW // per_tile) + j
                        z = layer * 4 * KT + m + n * KT
                        act.wait_ge(z_added, z + (2 + 1))
                        act.wait_ge(z_summed, z + 1)
                        A(zsq(j), x[:, bass.ds(m, 1), :].rearrange("p a s -> p (a s)"),
                          ACT.Square).then_inc(z_squared, 1)
                rounds(layer, s0, KT * per_tile, body)

            def root(layer, n):
                act.wait_ge(var_ready, layer * 4 + n + 1)
                A(small[:, 16:20], small[:, 12:16], ACT.Sqrt).then_inc(std_ready, 1)
                if n >= 2:
                    A(small[:, 46:47], small[:, 47:48], ACT.Silu)

            def affine(layer, n, k):
                act.wait_ge(y_centered, layer * 4 * KT + n * KT + k + 1)
                c = V_LN + 16 * n + k
                A(x[:, k, :], x[:, k, :], ACT.Identity, bias=vec(c + 8), scale=vec(c))
                act.drain()
                A(act_hi[:, k, :], x[:, k, :], ACT.Copy).then_inc(x_hi_made, 1)

            def ffn(layer, f, n):
                base = layer * (2 * FT) + f * FT

                def body(it, adv):
                    for j in range(2):
                        adv(2 * j)
                        act.wait_ge(h_made, base + it * 2 + (j + 1))
                        A(work[:, j, :], bank(2 * j), ACT.Silu).then_inc(gate_silu, 1)
                        adv(2 * j + 1)
                rounds(layer, S_IN[f], 2 * FT, body)
                squares(layer, n, S_OUT[f], 2)
                root(layer, n)
                for k in range(KT):
                    affine(layer, n, k)

            def mixer(layer):
                def read(kind, i):
                    step(layer, S_MIX + MIX_SLOT[kind, i])
                    return bank([t[0:2] for t in MIX_TILES].index((kind, i)) % 4)

                lm = vecs[:, V_LAM:V_LAM + AT]

                def l(n):
                    return lam[:, n * AT:(n + 1) * AT]

                A(l(0), lm, ACT.Abs)
                act.drain()
                A(l(1), l(0), ACT.Exp, scale=-1.0)
                act.drain()
                A(l(2), l(1), ACT.Ln, bias=1.0).then_inc(lam_log, 1)
                act.drain()
                A(l(3), l(2), ACT.Tanh, scale=0.5).then_inc(lam_tanh, 1)
                for t in range(AT):
                    A(xa_pad[:, t, RG_K - 1:], read("xa", t), ACT.Copy).then_inc(evac, 1)
                for t in range(CT):
                    A(CC[t], read("cg", t), ACT.Sigmoid).then_inc(evac, 1)
                for t in range(CT):
                    step(layer, S_MIX + MIX_SLOT["ca", t])
                for t in range(AT):
                    for g, (dst, c) in enumerate(((RR, V_BR), (II, V_BI))):
                        n = 2 * t + g
                        act.wait_ge(rg_gate_ready, layer * 6 + n + 1)
                        A(dst[t], bank(4 + n % 4), ACT.Sigmoid, bias=vec(c + t)).then_inc(
                            rg_gate_read, 1)
                act.drain()
                act.wait_ge(lam_ready, layer + 1)
                for t in range(AT):
                    A(TH[t], RR[t], ACT.Tanh, scale=l(11)[:, t:t + 1])
                for t in range(AT):
                    A(EE[t], RR[t], ACT.Exp, scale=l(12)[:, t:t + 1])
                act.drain()
                for t in range(AT):
                    A(RR[t], TH[t], ACT.Sqrt).then_inc(rg_factors, 1)
                for g in range(2):
                    A(KK[g], read("k", g), ACT.Copy).then_inc(evac, 1)
                for g in range(2):
                    A(QQ[g], read("q", g), ACT.Copy).then_inc(evac, 1)
                b = read("g", 0)
                A(lr, b[LR_ROW:LR_ROW + RANK, :], ACT.Copy)
                A(GG[0][0:DV, :], b[0:DV, :], ACT.Silu).then_inc(evac, 1)
                A(GG[1][0:DV, :], read("g", 1)[0:DV, :], ACT.Silu).then_inc(evac, 1)
                act.wait_ge(gla_gate_ready, layer + 1)
                for g in range(2):
                    A(GP[g], bank(6 + g), ACT.Identity, bias=vec(V_BG + g))
                    last = A(CU[g], bank(6 + g), ACT.Abs, bias=vec(V_BG + g))
                last.then_inc(gla_gate_read, 1)
                act.drain()
                for g in range(2):
                    A(CU[g], CU[g], ACT.Exp, scale=-1.0)
                act.drain()
                for g in range(2):
                    A(CU[g], CU[g], ACT.Ln, bias=1.0).then_inc(gla_log, 1)
                for s in range(2):
                    step(layer, S_MIX + V_SLOT + s)
                for t in range(TT):
                    A(v_tok[:, t, :], bank(4 + t, P, W_B), ACT.Copy).then_inc(evac, 1)
                for g in range(2):
                    act.wait_ge(gla_cum, layer * 2 + g + 1)
                    A(EB[g], CU[g], ACT.Exp, scale=1 / 16)
                    A(KI[g], CU[g], ACT.Exp, scale=-1 / 16)
                    A(GP[g], GP[g], ACT.Exp, scale=1 / 16).then_inc(gla_exp, 1)
                act.wait_ge(ktok_ready, layer + 1)
                A(k_tok[:, 0:2, :].rearrange("p t e -> p (t e)"), bank(6), ACT.Copy)
                A(k_tok[:, 2:4, :].rearrange("p t e -> p (t e)"), bank(7), ACT.Copy).then_inc(
                    ktok_read, 1)
                for i in (2, 3):
                    A(GG[i][0:DV, :], read("g", i)[0:DV, :], ACT.Silu).then_inc(evac, 1)

                def gelu(t):
                    if t == 0:
                        act.wait_ge(rg_scanned, layer * AT + AT)
                    A(YA[t], read("ya", t), ACT.Gelu_apprx_tanh).then_inc(evac, 1)

                def read_o(h):
                    act.wait_ge(o_ready, layer * HEADS + h + 1)
                    if h >= 2:
                        act.wait_ge(rms_ready, layer * HEADS + h - 1)
                    A(OO[h][0:DV, :], bank(6 + h % 2, DV), ACT.Copy)
                    A(OSQ[h % 2][0:DV, :], bank(6 + h % 2, DV), ACT.Square).then_inc(o_read, 1)

                gelu(0)
                read_o(0)
                read_o(1)
                gelu(1)
                gelu(2)

                def rms_sqrt(h):
                    act.wait_ge(rms_ready, layer * HEADS + h + 1)
                    if h >= 2:
                        act.wait_ge(mixed, layer * (AT + HEADS) + AT + h - 1)
                    A(RS[h % 2][0:DV, :], bank(h % 2, DV), ACT.Sqrt,
                      bias=small[0:DV, 47:48]).then_inc(rms_root, 1)

                def hi(k):
                    rows = DV if AT <= k < AT + HEADS else P
                    src = XC[k] if k < AT else OO[k - AT] if k < AT + HEADS else \
                        CC[k - AT - HEADS]
                    A(act_hi[0:rows, k, :], src[0:rows, :], ACT.Copy).then_inc(mixed_hi, 1)

                rms_sqrt(0)
                rms_sqrt(1)
                read_o(2)
                read_o(3)
                for t in range(AT):
                    act.wait_ge(mixed, layer * (AT + HEADS) + t + 1)
                    hi(t)
                for t in range(CT):
                    act.wait_ge(gn_centered, layer * CT + t + 1)
                    A(SQ[t], CC[t], ACT.Square).then_inc(gn_squared, 1)
                rms_sqrt(2)
                rms_sqrt(3)
                for t in range(CT):
                    act.wait_ge(gn_var, layer * CT + t + 1)
                    A(SQ[t], bank(2 + t), ACT.Sqrt, bias=small[:, 47:48]).then_inc(gn_root, 1)
                for h in range(HEADS):
                    act.wait_ge(mixed, layer * (AT + HEADS) + AT + h + 1)
                    hi(AT + h)
                for t in range(CT):
                    act.wait_ge(gn_scaled, layer * CT + t + 1)
                    A(CC[t], CC[t], ACT.Silu, scale=vec(V_GG + t), bias=vec(V_GB + t))
                    act.drain()
                    hi(AT + HEADS + t)
                act.wait_ge(mixed_split, layer * MIXK + MIXK)
                act.dma_start(mem_raw[:, :, :], mem_in).then_inc(mem_loaded, 16)
                act.wait_ge(mem_loaded, layer * 16 + 16)
                A(mem_hi[:, :, :], mem_raw[:, :, :], ACT.Copy).then_inc(mem_hi_made, 1)
                squares(layer, 1, S_MIXOUT, 1)

            def attention(layer):
                def read_k(m):
                    step(layer, S_KV + m)
                    A(k_st[:, m, :], bank(2 + m % 2, P, MEM), ACT.Copy).then_inc(kv_read, 1)

                read_k(0)
                read_k(1)
                root(layer, 1)
                read_k(2)
                for k in range(KT):
                    affine(layer, 1, k)
                    if k % 2 == 1 and k // 2 < 4:
                        read_k(3 + k // 2)
                read_k(7)
                for half in range(2):
                    for s in range(4):
                        step(layer, S_KV + 8 + 4 * half + s)
                    for m in range(2):
                        A(v_st[:, m, half * SEQ:(half + 1) * SEQ], bank(2 + m),
                          ACT.Copy).then_inc(kv_read, 1)
                act.wait_ge(kv_split, layer * 2 + 2)
                for m in range(KT):
                    step(layer, S_Q + m)
                    A(q_hi[:, m, :], bank(m % 4), ACT.Copy).then_inc(q_hi_made, 1)

                def exps(h):
                    act.wait_ge(max_ready, layer * XH + h + 1)
                    if h >= 2:
                        act.wait_ge(pT_ready, layer * XH + h - 1)
                    for t in range(TT):
                        last = A(probs[:, h % 2, t, :],
                                 psum[:, h % 2 * 2 + t // 2, t % 2 * MEM:(t % 2 + 1) * MEM],
                                 ACT.Exp, scale=XSCALE,
                                 bias=small[:, 24 + h % 2 * 4 + t:25 + h % 2 * 4 + t],
                                 accum_out=small[:, 32 + h % 2 * 4 + t:33 + h % 2 * 4 + t])
                    last.then_inc(exp_ready, 1)

                exps(0)
                for h in range(XH):
                    if h + 1 < XH:
                        exps(h + 1)
                    act.wait_ge(pT_ready, layer * XH + h + 1)
                    if h >= 1:
                        act.wait_ge(ctx_ready, layer * KT + 2 * h)
                    A(pT_hi[:, :, :], psum[:, 4:6, :], ACT.Copy).then_inc(pT_hi_made, 1)
                    for e in range(2):
                        act.wait_ge(ctx_ready, layer * KT + 2 * h + e + 1)
                        A(act_hi[:, 2 * h + e, :], bank(6 + e), ACT.Copy).then_inc(ctx_hi_made, 1)
                squares(layer, 2, S_AO, 1)
                root(layer, 2)
                for k in range(KT):
                    affine(layer, 2, k)

            with act.Fori(0, LAYERS) as layer:
                act.drain()
                act.dma_start(vecs[:, :], vecs_in[bass.ds(layer, 1)].rearrange(
                    "a p n -> (a p) n")).then_inc(vectors_loaded, 16)
                act.dma_start(mats[:, :], mats_in[bass.ds(layer, 1)].rearrange(
                    "a p n -> (a p) n")).then_inc(vectors_loaded, 16)
                act.wait_ge(vectors_loaded, layer * 32 + 32)
                ffn(layer, 0, 0)
                mixer(layer)
                attention(layer)
                ffn(layer, 1, 3)

        @block.vector
        def _(dve):
            V = nc.vector
            dve.sem_inc(h_made, 2)
            dve.sem_inc(z_added, 2)
            dve.sem_inc(z_summed, 2)
            dve.sem_inc(q_split, 4)
            V.memset(small[:, 47:48], EPS).then_inc(eps_set, 1)
            dve.wait_ge(consts_loaded, 16)
            dve.wait_ge(x_loaded, 16)

            def vec(c, rows=P):
                return vecs[0:rows, c:c + 1]

            def done(layer, s):
                dve.wait_ge(slot_multiplied, layer * SLOTS + s + (SPLIT + 1))

            def xt(it, j):
                return x[:, bass.ds(it * 2 + j, 1), :].rearrange("p a s -> p (a s)")

            def residual(layer, n, s0, per_tile, alpha):
                dve.drain()
                V.memset(work[:, 0:2, :], 0.0)
                with dve.Fori(0, KT // 2) as it:
                    for j in range(2):
                        z = layer * 4 * KT + it * 2 + (n * KT + j)
                        done(layer, it * (2 * per_tile) + (s0 + (j + 1) * per_tile - 1))
                        V.scalar_tensor_tensor(xt(it, j), xt(it, j), alpha, bank(j), ALU.mult,
                                               ALU.add).then_inc(z_added, 1)
                        dve.drain()
                        V.tensor_tensor(zsum, zsum, xt(it, j), ALU.add)
                        dve.wait_ge(z_squared, z + 1)
                        V.tensor_tensor(zsqsum, zsqsum, zsq(j), ALU.add).then_inc(z_summed, 1)

            def norm(layer, n, eps):
                dve.wait_ge(stats_ready, layer * 4 + n + 1)
                V.tensor_copy(small[:, 0:8], psum[:, 6, 0:8])
                dve.drain()
                V.tensor_tensor(small[:, 8:12], small[:, 0:4], small[:, 0:4], ALU.mult)
                dve.drain()
                V.tensor_tensor(small[:, 8:12], small[:, 4:8], small[:, 8:12], ALU.subtract)
                dve.drain()
                V.tensor_scalar(small[:, 12:16], small[:, 8:12], 0.0, eps, ALU.max,
                                ALU.add).then_inc(var_ready, 1)
                dve.wait_ge(std_ready, layer * 4 + n + 1)
                V.reciprocal(small[:, 8:12], small[:, 16:20])
                dve.drain()
                V.tensor_tensor(small[:, 8:12], small[:, 8:12], small[:, 12:16], ALU.mult)
                dve.drain()
                V.tensor_tensor(small[:, 8:12], small[:, 8:12], small[:, 16:20], ALU.add)
                dve.drain()
                V.reciprocal(small[:, 16:20], small[:, 8:12])
                dve.drain()
                V.tensor_tensor(small[:, 20:24], small[:, 0:4], small[:, 16:20], ALU.mult)
                dve.drain()
                for a in range(2):
                    for t in range(TT):
                        c = 16 + 4 * a + t
                        last = V.tensor_scalar(diag[:, a * TT + t, :], ident, small[:, c:c + 1],
                                               2.0, ALU.mult, ALU.mult)
                last.then_inc(diag_ready, 1)
                dve.wait_ge(bcast_ready, layer * 4 + n + 1)
                for k in range(KT):
                    V.tensor_tensor(x[:, k, :], x[:, k, :], bank(4), ALU.mult)
                    dve.drain()
                    V.tensor_tensor(x[:, k, :], x[:, k, :], bank(5),
                                    ALU.subtract).then_inc(y_centered, 1)

            def ffn(layer, f, n):
                base = layer * (2 * FT) + f * FT
                with dve.Fori(0, FT // 2) as it:
                    for j in range(2):
                        i = it * 2 + j
                        h = work[:, 2 + j, :]
                        hi = h_hi[:, bass.ds(i, 1), :].rearrange("p a s -> p (a s)")
                        lo = h_lo[:, bass.ds(i, 1), :].rearrange("p a s -> p (a s)")
                        done(layer, it * 4 + (S_IN[f] + 2 * j + 1))
                        dve.wait_ge(gate_silu, base + i + (2 + 1))
                        V.tensor_tensor(h, work[:, j, :], bank(2 * j + 1),
                                        ALU.mult).then_inc(h_made, 1)
                        dve.drain()
                        V.tensor_copy(hi, h)
                        dve.drain()
                        V.tensor_tensor(lo, h, hi.bitcast(F32), ALU.subtract).then_inc(h_split, 1)
                residual(layer, n, S_OUT[f], 2, 2 * ALPHA)
                norm(layer, n, 4 * EPS)

            def mixer(layer):
                def l(n):
                    return lam[:, n * AT:(n + 1) * AT]

                E = layer * EVACS
                dve.wait_ge(vectors_loaded, layer * 32 + 32)
                V.memset(xa_pad[:, :, 0:RG_K - 1], 0.0)
                V.memset(u_pad[:, :, 0:CONV_K - 1], 0.0)
                dve.wait_ge(lam_log, layer + 1)
                V.tensor_scalar(l(4), l(1), 2.0, None, ALU.add)
                dve.drain()
                V.reciprocal(l(5), l(4))
                dve.drain()
                V.tensor_tensor(l(6), l(1), l(5), ALU.mult)
                V.tensor_scalar(l(10), vecs[:, V_LAM:V_LAM + AT], -1.0, 0.0, ALU.mult, ALU.max)
                dve.wait_ge(lam_tanh, layer + 1)
                V.tensor_tensor(l(7), l(3), l(3), ALU.mult)
                dve.drain()
                V.tensor_tensor(l(8), l(6), l(3), ALU.subtract)
                V.tensor_scalar(l(7), l(7), -1.0, 1.0, ALU.mult, ALU.add)
                dve.drain()
                V.reciprocal(l(9), l(7))
                dve.drain()
                V.tensor_tensor(l(9), l(9), l(8), ALU.mult)
                dve.drain()
                V.scalar_tensor_tensor(l(9), l(9), 2.0, l(2), ALU.mult, ALU.add)
                dve.drain()
                V.tensor_tensor(l(9), l(9), l(10), ALU.add)
                dve.drain()
                V.tensor_scalar(l(11), l(9), 4.0, None, ALU.mult)
                V.tensor_scalar(l(12), l(9), -8.0, None, ALU.mult).then_inc(lam_ready, 1)

                for t in range(AT):
                    dve.wait_ge(evac, E + EV["xa", t])
                    V.tensor_scalar(XC[t], xa_pad[:, t, RG_K - 1:],
                                    vec(V_CW + (RG_K - 1) * AT + t), vec(V_CB + t),
                                    ALU.mult, ALU.add)
                    for j in range(RG_K - 1):
                        dve.drain()
                        last = V.scalar_tensor_tensor(XC[t], xa_pad[:, t, j:j + SEQ],
                                                      vec(V_CW + j * AT + t), XC[t],
                                                      ALU.mult, ALU.add)
                    last.then_inc(xc_ready, 1)
                for t in range(CT):
                    done(layer, S_MIX + MIX_SLOT["ca", t])
                    dve.wait_ge(evac, E + EV["cg", t])
                    b = [m[0:2] for m in MIX_TILES].index(("ca", t)) % 4
                    V.tensor_tensor(u_pad[:, t, CONV_K - 1:], CC[t], bank(b),
                                    ALU.mult).then_inc(ca_used, 1)

                def taps(t, j0, j1):
                    for j in range(j0, j1):
                        dve.drain()
                        w = vec(V_DW + j * CT + t)
                        if j == 0:
                            last = V.tensor_scalar(CC[t], u_pad[:, t, 0:SEQ], w, vec(V_DB + t),
                                                   ALU.mult, ALU.add)
                        else:
                            last = V.scalar_tensor_tensor(CC[t], u_pad[:, t, j:j + SEQ], w, CC[t],
                                                          ALU.mult, ALU.add)
                    if j1 == CONV_K:
                        last.then_inc(conv_done, 1)

                taps(0, 0, CONV_K)
                for t in range(AT):
                    dve.wait_ge(rg_factors, layer * AT + t + 1)
                    V.scalar_tensor_tensor(TH[t], EE[t], 1.0, TH[t], ALU.add, ALU.mult)
                    V.scalar_tensor_tensor(RR[t], EE[t], 1.0, RR[t], ALU.add, ALU.mult)
                    V.tensor_tensor(II[t], II[t], XC[t], ALU.mult)
                    dve.drain()
                    V.tensor_scalar(TH[t], TH[t], -1.0, 1.0, ALU.mult, ALU.add)
                    V.tensor_tensor(RR[t], RR[t], II[t], ALU.mult)
                    dve.drain()
                    V.tensor_tensor_scan(XC[t], TH[t], RR[t], 0.0, ALU.mult,
                                         ALU.add).then_inc(rg_scanned, 1)
                for g in range(2):
                    dve.wait_ge(gla_log, layer * 2 + g + 1)
                    V.scalar_tensor_tensor(GP[g], GP[g], 0.0, CU[g], ALU.min, ALU.subtract)
                    dve.drain()
                    V.tensor_tensor_scan(CU[g], not_start, GP[g], 0.0, ALU.mult, ALU.add)
                    dve.drain()
                    c = CU[g].rearrange("p (n c) -> p n c", c=CHUNK)
                    V.tensor_tensor(GP[g].rearrange("p (n c) -> p n c", c=CHUNK),
                                    c[:, :, CHUNK - 1:CHUNK].to_broadcast([P, NCHUNK, CHUNK]), c,
                                    ALU.subtract).then_inc(gla_cum, 1)
                dve.wait_ge(evac, E + EV["q", 1])
                V.memset(tmp[:, 37 * SEQ:39 * SEQ], 0.0)
                for g in range(2):
                    dve.wait_ge(gla_exp, layer * 2 + g + 1)
                    V.scalar_tensor_tensor(QQ[g], QQ[g], DK ** -0.5, EB[g], ALU.mult, ALU.mult)
                    V.tensor_tensor(KI[g], KK[g], KI[g], ALU.mult)
                    V.tensor_tensor(GP[g], KK[g], GP[g], ALU.mult).then_inc(gla_qk, 1)
                for n in range(NCHUNK - 1):
                    dve.drain()
                    dve.wait_ge(u_ready, layer * (NCHUNK - 1) + n + 1)
                    for g in range(2):
                        for r in range(2):
                            rows = slice(r * CHUNK, (r + 1) * CHUNK)
                            c = (2 * g + r) * DV
                            u = psum[rows, 4 + n % 2, c:c + DV]
                            if n == 0:
                                last = V.tensor_copy(state[rows, 1, g, :], u)
                            else:
                                e = (n + 1) * CHUNK - 1
                                last = V.scalar_tensor_tensor(
                                    state[rows, n + 1, g, :], state[rows, n, g, :],
                                    EB[g][rows, e:e + 1], u, ALU.mult, ALU.add)
                    last.then_inc(state_ready, 1)

                def mask(h):
                    dve.wait_ge(score_ready, layer * HEADS + h + 1)
                    if h >= 2:
                        dve.wait_ge(o_ready, layer * HEADS + h - 1)
                    dve.sem_inc(dve_wait_carrier, 1)
                    m = score_mask.rearrange("p (a c) -> p a c", a=1).to_broadcast([P, TT, P])
                    V.copy_predicated(SC[h % 2].rearrange("p (t c) -> p t c", c=P), m,
                                      bank(4 + h % 2).rearrange("p (t c) -> p t c", c=P)
                                      ).then_inc(score_masked, 1)

                mask(0)
                mask(1)
                taps(1, 0, 12)
                mask(2)
                taps(1, 12, 20)
                mask(3)
                taps(1, 20, CONV_K)
                for t in range(AT):
                    dve.wait_ge(evac, E + EV["ya", t])
                    V.tensor_tensor(XC[t], XC[t], YA[t], ALU.mult).then_inc(mixed, 1)
                for t in range(CT):
                    dve.wait_ge(gn_mean, layer * CT + t + 1)
                    V.tensor_tensor(CC[t], CC[t], bank(2 + t), ALU.subtract).then_inc(
                        gn_centered, 1)
                for h in range(HEADS):
                    rs, o = RS[h % 2][0:DV, :], OO[h][0:DV, :]
                    dve.wait_ge(rms_root, layer * HEADS + h + 1)
                    V.reciprocal(rs, rs)
                    dve.drain()
                    V.scalar_tensor_tensor(o, o, vec(V_NG, DV), rs, ALU.mult, ALU.mult)
                    dve.drain()
                    V.tensor_tensor(o, o, GG[h][0:DV, :], ALU.mult).then_inc(mixed, 1)
                for t in range(CT):
                    dve.wait_ge(gn_root, layer * CT + t + 1)
                    V.reciprocal(SQ[t], SQ[t])
                    dve.drain()
                    V.tensor_tensor(CC[t], CC[t], SQ[t], ALU.mult).then_inc(gn_scaled, 1)
                dve.wait_ge(mem_hi_made, layer + 1)
                V.tensor_tensor(mem_lo[:, :, :], mem_raw[:, :, :], mem_hi[:, :, :].bitcast(F32),
                                ALU.subtract).then_inc(mem_split, 1)
                residual(layer, 1, S_MIXOUT, 1, ALPHA)

            def attention(layer):
                norm(layer, 1, EPS)
                for n, (st, hi, lo) in enumerate(((k_st, kT_hi, kT_lo), (v_st, v_hi, v_lo))):
                    dve.wait_ge(kv_read, layer * 12 + (8, 12)[n])
                    V.tensor_copy(hi[:, :, :], st[:, :, :])
                    dve.drain()
                    V.tensor_tensor(lo[:, :, :], st[:, :, :], hi[:, :, :].bitcast(F32),
                                    ALU.subtract).then_inc(kv_split, 1)
                for m in range(KT):
                    dve.wait_ge(q_hi_made, layer * KT + m + 1)
                    V.tensor_tensor(q_lo[:, m, :], bank(m % 4), q_hi[:, m, :].bitcast(F32),
                                    ALU.subtract).then_inc(q_split, 1)

                def maxes(h):
                    dve.wait_ge(qk_ready, layer * XH + h + 1)
                    c = 24 + h % 2 * 4
                    V.reduce_max(small[:, 40:44], psum[:, h % 2 * 2:h % 2 * 2 + 2, :].rearrange(
                        "p a (t m) -> p (a t) m", m=MEM), AX.X)
                    dve.drain()
                    V.tensor_scalar(small[:, c:c + 4], small[:, 40:44], -XSCALE, None,
                                    ALU.mult).then_inc(max_ready, 1)

                maxes(0)
                for h in range(XH):
                    c = 32 + h % 2 * 4
                    dve.wait_ge(exp_ready, layer * XH + h + 1)
                    V.reciprocal(small[:, c:c + 4], small[:, c:c + 4])
                    dve.drain()
                    for t in range(TT):
                        last = V.tensor_scalar(probs[:, h % 2, t, :], probs[:, h % 2, t, :],
                                               small[:, c + t:c + t + 1], None, ALU.mult)
                    last.then_inc(probs_ready, 1)
                    if h + 1 < XH:
                        maxes(h + 1)
                    dve.wait_ge(pT_hi_made, layer * XH + h + 1)
                    V.tensor_tensor(pT_lo[:, :, :], psum[:, 4:6, :], pT_hi[:, :, :].bitcast(F32),
                                    ALU.subtract).then_inc(pT_split, 1)
                    for e in range(2):
                        dve.wait_ge(ctx_hi_made, layer * KT + 2 * h + e + 1)
                        V.tensor_tensor(act_lo[:, 2 * h + e, :], bank(6 + e),
                                        act_hi[:, 2 * h + e, :].bitcast(F32),
                                        ALU.subtract).then_inc(ctx_split, 1)
                residual(layer, 2, S_AO, 1, ALPHA)
                norm(layer, 2, EPS)

            with dve.Fori(0, LAYERS) as layer:
                ffn(layer, 0, 0)
                mixer(layer)
                attention(layer)
                ffn(layer, 1, 3)


def kernel(**inputs):
    import numpy as np
    import concourse.bacc as bacc
    from concourse.bass_utils import run_bass_kernel_spmd as run

    a = {k: np.asarray(v) for k, v in inputs.items()}
    L = LAYERS
    f32 = np.float32

    def tiles(w, kt=KT):
        n = w.shape[2] // P
        return np.ascontiguousarray(
            w.reshape(L, kt, P, n, P).transpose(0, 3, 2, 1, 4)).reshape(L * n, P, kt * P)

    def ffn_in(w):
        w = w.reshape(L, KT, P, 2, FT, P).transpose(0, 4, 3, 2, 1, 5)
        return np.ascontiguousarray(w).reshape(L * 2 * FT, P, KT * P)

    def ffn_out(w):
        w = w.reshape(L, 2, FT // 2, P, KT, P).transpose(0, 4, 1, 3, 2, 5)
        return np.ascontiguousarray(w).reshape(L * 2 * KT, P, FT // 2 * P)

    m = a["mix_w_in"]
    xa, ya = m[:, :, 0:384], m[:, :, 384:768]
    q, k = m[:, :, 768:960], m[:, :, 960:1152]
    v, g, lrw = m[:, :, 1152:1536], m[:, :, 1536:1920], m[:, :, 1920:1936]
    ca, cg = m[:, :, 1936:2192], m[:, :, 2192:2448]

    def pairs(w):
        o = np.zeros(w.shape[:-1] + (2 * P,), f32)
        for h in range(HEADS):
            o[..., h * CHUNK:h * CHUNK + DK] = w[..., h * DK:(h + 1) * DK]
        return o

    gg = np.zeros((L, D, HEADS * P), f32)
    for h in range(HEADS):
        gg[:, :, h * P:h * P + DV] = g[:, :, h * DV:(h + 1) * DV]
    gg[:, :, LR_ROW:LR_ROW + RANK] = lrw
    parts = {"xa": xa, "ya": ya, "k": pairs(k), "q": pairs(q), "g": gg, "ca": ca, "cg": cg}
    w_mix = tiles(np.concatenate([parts[n][:, :, i * P:(i + 1) * P] for n, i, _, _ in MIX_TILES], 2))
    w_v = np.ascontiguousarray(v.reshape(L, 2, 4, P, W_B).transpose(0, 1, 3, 2, 4)).reshape(
        L * 2, P, 4 * W_B)
    mo = np.zeros((L, MIXK * P, D), f32)
    src = a["mix_w_out"]
    mo[:, 0:W_A] = src[:, 0:W_A]
    for h in range(HEADS):
        mo[:, (AT + h) * P:(AT + h) * P + DV] = src[:, W_A + h * DV:W_A + (h + 1) * DV]
    mo[:, (AT + HEADS) * P:] = src[:, W_A + W_B:]
    kv = a["xa_w_kv"]
    w_vm = kv[:, :, D:].reshape(L, 4, 2, P, 2, SEQ).transpose(0, 4, 1, 3, 2, 5).reshape(
        L, 8, P, 8 * P)
    w_kv = np.concatenate([tiles(kv[:, :, 0:D]).reshape(L, 8, P, 8 * P), w_vm], 1).reshape(
        L * 16, P, 8 * P)

    def cols(w, n):
        return w.reshape(L, n, P).transpose(0, 2, 1)

    vecs = np.zeros((L, P, NV), f32)
    for s in range(4):
        vecs[:, :, V_LN + 16 * s:V_LN + 16 * s + 8] = cols(a[f"ln{s + 1}_g"], KT)
        vecs[:, :, V_LN + 16 * s + 8:V_LN + 16 * s + 16] = cols(a[f"ln{s + 1}_b"], KT)
    for j in range(RG_K):
        vecs[:, :, V_CW + j * AT:V_CW + (j + 1) * AT] = cols(a["rg_conv_w"][:, j], AT)
    for c, n in ((V_CB, "rg_conv_b"), (V_BR, "rg_b_r"), (V_BI, "rg_b_i"), (V_LAM, "rg_lambda")):
        vecs[:, :, c:c + AT] = cols(a[n], AT)
    vecs[:, :, V_BG:V_BG + 2] = cols(pairs(a["gla_b_gate"]), 2)
    vecs[:, 0:DV, V_NG] = a["gla_norm_g"]
    for j in range(CONV_K):
        vecs[:, :, V_DW + j * CT:V_DW + (j + 1) * CT] = cols(a["cv_dw_w"][:, j], CT)
    for c, n in ((V_DB, "cv_dw_b"), (V_GG, "cv_gn_g"), (V_GB, "cv_gn_b")):
        vecs[:, :, c:c + CT] = cols(a[n], CT)
    mats = np.zeros((L, P, 1024), f32)
    for g_, n in enumerate(("rg_w_r", "rg_w_i")):
        for b in range(W_A // 64):
            r = b % 2 * 64
            c = (AT * g_ + b // 2) * P + r
            mats[:, r:r + 64, c:c + 64] = a[n][:, b]
    mats[:, LR_ROW:LR_ROW + RANK, 2 * AT * P:] = pairs(a["gla_w_gate"])

    consts = np.zeros((P, NC_), f32)
    idx = np.arange(P)
    consts[:, C_ID:C_ID + P] = np.eye(P, dtype=f32)
    consts[:, C_ONE:C_ONE + P] = 1.0
    same = idx[:, None] // 64 == idx[None, :] // 64
    consts[:, C_B64:C_B64 + P] = np.where(same, f32(1 / 64), f32(0))
    consts[:, C_O96:C_O96 + P] = 1 / DV
    consts[:, C_MASK:C_MASK + P] = np.where(same & (idx[:, None] <= idx[None, :]), f32(1), f32(0))
    consts[:, C_START:C_START + SEQ] = np.where(np.arange(SEQ) % CHUNK == 0, f32(0), f32(1))
    consts[:, C_AVG] = 1 / D

    def features(t):
        return np.ascontiguousarray(t.T.reshape(KT, P, t.shape[0]).transpose(1, 0, 2))

    arrays = {
        "x_in": features(a["x"][0]), "mem_in": features(a["mem"][0]), "consts_in": consts,
        "vecs_in": vecs, "mats_in": mats,
        "w_in1": ffn_in(a["ffn1_w_in"]), "w_out1": ffn_out(a["ffn1_w_out"]),
        "w_in2": ffn_in(a["ffn2_w_in"]), "w_out2": ffn_out(a["ffn2_w_out"]),
        "w_mix": w_mix, "w_v": w_v, "w_mixout": tiles(mo, MIXK), "w_kv": w_kv,
        "w_q": tiles(a["xa_w_q"]), "w_o": tiles(a["xa_w_o"]),
    }
    nc = bacc.Bacc("TRN2", target_bir_lowering=False, num_devices=1)
    args = [nc.dram_tensor(n, t.shape, mybir.dt.from_np(t.dtype), kind="ExternalInput").ap()
            for n, t in arrays.items()]
    out = nc.dram_tensor("out", (P, KT, SEQ), F32, kind="ExternalOutput").ap()
    hybrid_decoder(nc, *args, out)
    r = run(nc, [arrays], core_ids=[0])
    got = r.results[0]["out"]
    return np.ascontiguousarray(got.transpose(1, 0, 2).reshape(D, SEQ).T)[None]
```

```python
import concourse.bass as bass
from concourse import mybir
from contextlib import ExitStack

F32 = mybir.dt.float32
F32R = mybir.dt.float32r
U32 = mybir.dt.uint32
ALU = mybir.AluOpType
ACT = mybir.ActivationFunctionType
AX = mybir.AxisListType

LAYERS = 2
SEQ = 512
D = 1024
MEM = 256
D_FF = 2816
P = 128
KT = D // P
FT = D_FF // P
TT = SEQ // P
ALPHA = (2.0 * LAYERS) ** 0.25
EPS = 1e-5

W_A, W_B, W_C = 384, 384, 256
AT, CT = W_A // P, W_C // P
RG_K, CONV_K = 4, 31
HEADS, DK, DV, RANK, CHUNK = 4, 48, 96, 16, 64
NCHUNK = SEQ // CHUNK
LR_ROW = DV
MIXK = AT + HEADS + CT
XH, XD = 4, 256
XSCALE = XD ** -0.5

UNITS = 12
RAW, SPLIT = 4, 2
S_IN = (0, 120)
S_OUT = (44, 164)
S_MIX, S_MIXOUT, S_KV, S_Q, S_AO = 60, 80, 88, 104, 112
SLOTS = 180
V_SLOT = 13


def slot_width(s):
    if S_OUT[0] <= s < S_MIX or s >= S_OUT[1]:
        return FT // 2 * P
    if S_MIX + V_SLOT <= s < S_MIX + V_SLOT + 2:
        return 4 * W_B
    if S_MIXOUT <= s < S_KV:
        return MIXK * P
    return KT * P


V_LN = 0
V_CW = 64
V_CB = V_CW + RG_K * AT
V_BR = V_CB + AT
V_BI = V_BR + AT
V_LAM = V_BI + AT
V_BG = V_LAM + AT
V_NG = V_BG + 2
V_DW = V_NG + 1
V_DB = V_DW + CONV_K * CT
V_GG = V_DB + CT
V_GB = V_GG + CT
NV = V_GB + CT

C_ID, C_ONE, C_B64, C_O96, C_MASK, C_START, C_AVG = 0, 128, 256, 384, 512, 640, 1152
NC_ = 1153

MIX_TILES = [("xa", 0, 0, 0), ("xa", 1, 0, 0), ("xa", 2, 0, 0), ("cg", 0, 0, 0), ("cg", 1, 1, 0),
             ("ca", 0, 2, 0), ("ca", 1, 3, 0), ("k", 0, 4, 0), ("k", 1, 5, 0), ("q", 0, 0, 1),
             ("g", 0, 0, 2), ("q", 1, 6, 0), ("g", 1, 7, 0), ("g", 2, 8, 0), ("g", 3, 9, 0),
             ("ya", 0, 10, 0), ("ya", 1, 11, 0), ("ya", 2, 16, 0)]
MIX_SLOT = {(k, i): n if n < 13 else n + 2 for n, (k, i, _, _) in enumerate(MIX_TILES)}
EVAC = ([("xa", 0), ("xa", 1), ("xa", 2), ("cg", 0), ("cg", 1), ("k", 0), ("k", 1), ("q", 0),
         ("g", 0), ("q", 1), ("g", 1)] + [("v", t) for t in range(4)] +
        [("g", 2), ("g", 3), ("ya", 0), ("ya", 1), ("ya", 2)])
EVACS = len(EVAC)
EV = {e: n + 1 for n, e in enumerate(EVAC)}
MIX_ORDER = [("r", 0), ("r", 1), ("c", 0), ("c", 1), ("h", 0), ("h", 1), ("r", 2), ("h", 2),
             ("h", 3)]
GN_BANK = (2, 1)
V_BANK = (4, 2)


def hybrid_decoder(nc, x_in, mem_in, consts_in, vecs_in, mats_in, w_in1, w_out1, w_in2, w_out2,
                   w_mix, w_v, w_mixout, w_kv, w_q, w_o, out):
    ctx = ExitStack()
    with ctx:
        def sb(name, shape, dt=F32):
            return ctx.enter_context(nc.sbuf_tensor(name, shape, dt))

        def sem(name):
            return ctx.enter_context(nc.semaphore(name))

        x = sb("x", [P, KT, SEQ])
        act_hi = sb("act_hi", [P, MIXK, SEQ], F32R)
        act_lo = sb("act_lo", [P, MIXK, SEQ], F32R)
        raw = sb("raw", [P, RAW, UNITS * P])
        w_hi = sb("w_hi", [P, SPLIT, UNITS * P], F32R)
        w_lo = sb("w_lo", [P, SPLIT, UNITS * P], F32R)
        work = sb("work", [P, 4, SEQ])
        consts = sb("consts", [P, NC_])
        vecs = sb("vecs", [P, NV])
        mats = sb("mats", [P, 1024])
        small = sb("small", [P, 48])
        small_split = sb("small_split", [P, 16], F32R)
        ident_r = sb("ident_r", [P, P], F32R)
        lam = sb("lam", [P, 13 * AT])

        with ExitStack() as part:
            h_hi = part.enter_context(nc.sbuf_tensor("h_hi", [P, FT, SEQ], F32R))
            h_lo = part.enter_context(nc.sbuf_tensor("h_lo", [P, FT, SEQ], F32R))
        with ExitStack() as part:
            tmp = part.enter_context(nc.sbuf_tensor("tmp", [P, 2 * FT * SEQ], F32))
        with ExitStack() as part:
            kT_hi = part.enter_context(nc.sbuf_tensor("kT_hi", [P, KT, MEM], F32R))
            kT_lo = part.enter_context(nc.sbuf_tensor("kT_lo", [P, KT, MEM], F32R))
            v_hi = part.enter_context(nc.sbuf_tensor("v_hi", [P, 2, D], F32R))
            v_lo = part.enter_context(nc.sbuf_tensor("v_lo", [P, 2, D], F32R))
            with ExitStack() as inner:
                mem_raw = inner.enter_context(nc.sbuf_tensor("mem_raw", [P, KT, MEM], F32))
                mem_hi = inner.enter_context(nc.sbuf_tensor("mem_hi", [P, KT, MEM], F32R))
                mem_lo = inner.enter_context(nc.sbuf_tensor("mem_lo", [P, KT, MEM], F32R))
                with ExitStack() as last:
                    k_st = last.enter_context(nc.sbuf_tensor("k_st", [P, KT, MEM], F32))
                    v_st = last.enter_context(nc.sbuf_tensor("v_st", [P, 2, D], F32))
                q_hi = inner.enter_context(nc.sbuf_tensor("q_hi", [P, KT, SEQ], F32R))
                q_lo = inner.enter_context(nc.sbuf_tensor("q_lo", [P, KT, SEQ], F32R))
            with ExitStack() as inner:
                probs = inner.enter_context(nc.sbuf_tensor("probs", [P, 2, TT, MEM], F32))
                pT_hi = inner.enter_context(nc.sbuf_tensor("pT_hi", [P, 2, SEQ], F32R))
                pT_lo = inner.enter_context(nc.sbuf_tensor("pT_lo", [P, 2, SEQ], F32R))
        region_end = ctx.enter_context(nc.sbuf_tensor("region", [P, 2 * FT * SEQ], F32))

        psum = ctx.enter_context(nc.psum_tensor("psum", [P, 8, SEQ], F32))

        ident = consts[:, C_ID:C_ID + P]
        ones = consts[:, C_ONE:C_ONE + P]
        block64 = consts[:, C_B64:C_B64 + P]
        ones96 = consts[0:DV, C_O96:C_O96 + DV]
        score_mask = consts[:, C_MASK:C_MASK + P].bitcast(U32)
        not_start = consts[:, C_START:C_START + SEQ]
        average = consts[:, C_AVG:C_AVG + 1]

        zsum, zsqsum = work[:, 0, :], work[:, 1, :]

        def zsq(m):
            return work[:, 2 + m % 2, :]

        def tile(n):
            return tmp[:, n * SEQ:(n + 1) * SEQ]

        XA_W, U_W = SEQ + RG_K - 1, SEQ + CONV_K - 1
        xa_pad = tmp[:, 0:AT * XA_W].rearrange("p (t s) -> p t s", t=AT)
        u_pad = tmp[:, AT * XA_W:AT * XA_W + CT * U_W].rearrange("p (t s) -> p t s", t=CT)
        XC = [tile(6 + t) for t in range(AT)]
        RR = [tile(9 + t) for t in range(AT)]
        II = [tile(12 + t) for t in range(AT)]
        EE = [tile(15 + t) for t in range(AT)]
        TH = [xa_pad[:, t, 0:SEQ] for t in range(AT)]
        CC = [tile(18 + t) for t in range(CT)]
        SQ = [u_pad[:, t, 0:SEQ] for t in range(CT)]
        KK = [tile(20 + t) for t in range(2)]
        QQ = [tile(22 + t) for t in range(2)]
        GP = [tile(24 + t) for t in range(2)]
        CU = [tile(26 + t) for t in range(2)]
        EB = [tile(28 + t) for t in range(2)]
        KI = [tile(30 + t) for t in range(2)]
        v_tok = tmp[:, 32 * SEQ:35 * SEQ].rearrange("p (t e) -> p t e", t=TT)
        k_tok = tmp[:, 35 * SEQ:37 * SEQ].rearrange("p (t e) -> p t e", t=TT)
        SC = [tile(37 + t) for t in range(2)]
        lr = tile(37)[LR_ROW:LR_ROW + RANK, :]
        state = tmp[:, 39 * SEQ:42 * SEQ].rearrange("p (n g e) -> p n g e", n=NCHUNK, g=2)
        GG = [tile(42), tile(43), tile(20), tile(21)]
        YA = EE
        OO = [tile(9), tile(10), tile(11), tile(12)]
        OSQ = CU + EB
        RS = [tile(13), tile(14)]

        def mixed_tile(k):
            kind, i = MIX_ORDER[k]
            t = {"r": XC, "c": CC, "h": OO}[kind][i]
            return t[0:DV, :] if kind == "h" else t

        def mixed_rows(k):
            return DV if MIX_ORDER[k][0] == "h" else P

        consts_loaded = sem("consts_loaded")
        x_loaded = [sem(f"x_loaded{part}") for part in range(4)]
        vectors_loaded, mem_loaded = sem("vectors_loaded"), sem("mem_loaded")
        raw_loaded = [sem(f"raw_loaded{j}") for j in range(RAW)]
        w_hi_made = sem("w_hi_made")
        slot_split = sem("slot_split")
        slot_multiplied = sem("slot_multiplied")
        eps_set = sem("eps_set")
        x_hi_made = sem("x_hi_made")
        x_split = sem("x_split")
        gate_silu = sem("gate_silu")
        h_made = sem("h_made")
        h_split = sem("h_split")
        z_added = sem("z_added")
        z_squared = sem("z_squared")
        z_summed = sem("z_summed")
        stats_ready = sem("stats_ready")
        var_ready = sem("var_ready")
        std_ready = sem("std_ready")
        scalars_split = sem("scalars_split")
        ident_made = sem("ident_made")
        bcast_ready = sem("bcast_ready")
        y_centered = sem("y_centered")
        evac = sem("evac")
        ca_used = sem("ca_used")
        lam_log, lam_q, lam_tanh, lam_ready = (sem("lam_log"), sem("lam_q"), sem("lam_tanh"),
                                               sem("lam_ready"))
        xc_ready = sem("xc_ready")
        rg_gate_ready = sem("rg_gate_ready")
        rg_gate_read = sem("rg_gate_read")
        rg_factors = sem("rg_factors")
        rg_scanned = sem("rg_scanned")
        gla_gate_ready = sem("gla_gate_ready")
        gla_gate_read = sem("gla_gate_read")
        gla_log = sem("gla_log")
        gla_cum = sem("gla_cum")
        gla_exp = sem("gla_exp")
        gla_qk = sem("gla_qk")
        ktok_ready, ktok_read = sem("ktok_ready"), sem("ktok_read")
        u_ready, state_ready = sem("u_ready"), sem("state_ready")
        score_ready, score_masked = sem("score_ready"), sem("score_masked")
        o_ready, o_read = sem("o_ready"), sem("o_read")
        rms_ready, rms_root = sem("rms_ready"), sem("rms_root")
        conv_done = sem("conv_done")
        gn_mean, gn_centered, gn_squared = sem("gn_mean"), sem("gn_centered"), sem("gn_squared")
        gn_var, gn_root, gn_scaled = sem("gn_var"), sem("gn_root"), sem("gn_scaled")
        rg_mixed, head_mixed = sem("rg_mixed"), sem("head_mixed")
        mixed_hi, mixed_split = sem("mixed_hi"), sem("mixed_split")
        mem_hi_made, mem_split = sem("mem_hi_made"), sem("mem_split")
        kv_read = sem("kv_read")
        kv_split = sem("kv_split")
        q_hi_made, q_split = sem("q_hi_made"), sem("q_split")
        qk_ready = sem("qk_ready")
        max_ready = sem("max_ready")
        exp_ready = sem("exp_ready")
        probs_ready = sem("probs_ready")
        pT_ready, pT_hi_made, pT_split = sem("pT_ready"), sem("pT_hi_made"), sem("pT_split")
        ctx_ready, ctx_hi_made, ctx_split = sem("ctx_ready"), sem("ctx_hi_made"), sem("ctx_split")
        out_stored = sem("out_stored")
        pool_wait_carrier, dve_wait_carrier = sem("pool_wait_carrier"), sem("dve_wait_carrier")

        def bank(b, rows=P, cols=SEQ):
            return psum[0:rows, b, 0:cols]

        block = ctx.enter_context(nc.Block())

        @block.sync
        def _(sp):
            def load(dram, layer, s, i, j, per_layer, width):
                sp.wait_ge(slot_split, layer * SLOTS + s + 1)
                src = dram[bass.ds(layer * per_layer + i, 1)].rearrange("a p n -> (a p) n")
                sp.dma_start(raw[:, j, 0:width], src).then_inc(raw_loaded[j], 16)

            def stage(dram, layer, s0, n, width):
                with sp.Fori(0, n // RAW) as it:
                    for j in range(RAW):
                        load(dram, layer, it * RAW + (s0 + j), it * RAW + j, j, n, width)

            with sp.Fori(0, LAYERS) as layer:
                stage(w_in1, layer, S_IN[0], 44, 8 * P)
                stage(w_out1, layer, S_OUT[0], 16, 11 * P)
                for s in range(20):
                    if V_SLOT <= s < V_SLOT + 2:
                        load(w_v, layer, S_MIX + s, s - V_SLOT, s % RAW, 2, 12 * P)
                    else:
                        i = s if s < V_SLOT else s - 2
                        load(w_mix, layer, S_MIX + s, i, s % RAW, 18, 8 * P)
                for s in range(8):
                    if s == RAW:
                        sp.wait_ge(mixed_split, layer * MIXK + MIXK)
                        sp.dma_start(mem_raw[:, :, :], mem_in).then_inc(mem_loaded, 16)
                    load(w_mixout, layer, S_MIXOUT + s, s, s % RAW, 8, MIXK * P)
                stage(w_kv, layer, S_KV, 16, 8 * P)
                stage(w_q, layer, S_Q, 8, 8 * P)
                stage(w_o, layer, S_AO, 8, 8 * P)
                stage(w_in2, layer, S_IN[1], 44, 8 * P)
                stage(w_out2, layer, S_OUT[1], 16, 11 * P)
            for part in range(4):
                sp.wait_ge(x_hi_made, KT + LAYERS * 4 * KT - KT + 2 * (part + 1))
                sp.dma_start(out[:, 2 * part:2 * part + 2, :],
                             x[:, 2 * part:2 * part + 2, :]).then_inc(out_stored, 16)
            sp.wait_ge(out_stored, 64)

        @block.gpsimd
        def _(pool):
            pool.sem_inc(slot_split, RAW)

            def split(layer, s, j, width):
                pool.wait_ge(w_hi_made, layer * (SLOTS - 2) + s - 1)
                r = j % SPLIT
                nc.gpsimd.tensor_tensor(w_lo[:, r, 0:width], raw[:, j, 0:width],
                                        w_hi[:, r, 0:width].bitcast(F32),
                                        ALU.subtract).then_inc(slot_split, 1)

            def split_first(layer, s):
                pool.wait_ge(raw_loaded[s], (layer * (SLOTS // RAW) + 1) * 16)
                pool.wait_ge(slot_multiplied, layer * SLOTS + s + 1)
                pool.sem_inc(pool_wait_carrier, 1)
                src = raw[:, s, 0:KT * P]
                nc.gpsimd.tensor_copy(w_hi[:, s, 0:KT * P], src)
                pool.drain()
                nc.gpsimd.tensor_tensor(w_lo[:, s, 0:KT * P], src,
                                        w_hi[:, s, 0:KT * P].bitcast(F32),
                                        ALU.subtract).then_inc(slot_split, 1)

            def rest(layer, s0, n, first):
                with pool.Fori(first, n // RAW) as it:
                    for j in range(RAW):
                        split(layer, it * RAW + (s0 + j), j, slot_width(s0))

            def split_x(layer, c):
                for k in range(KT):
                    pool.wait_ge(x_hi_made, layer * 4 * KT + c * KT + k + 1)
                    nc.gpsimd.tensor_tensor(act_lo[:, k, :], x[:, k, :],
                                            act_hi[:, k, :].bitcast(F32),
                                            ALU.subtract).then_inc(x_split, 1)

            def ffn(layer, f, c):
                s0 = S_IN[f]
                for j in range(RAW):
                    if j == SPLIT:
                        split_x(layer, c)
                    if f == 0 and j < SPLIT:
                        split_first(layer, j)
                    else:
                        split(layer, s0 + j, j, slot_width(s0))
                rest(layer, s0, 44, 1)
                rest(layer, S_OUT[f], 16, 0)

            with pool.Fori(0, LAYERS) as layer:
                ffn(layer, 0, 0)
                for s in range(20):
                    if s == SPLIT:
                        split_x(layer, 1)
                    split(layer, S_MIX + s, s % RAW, slot_width(S_MIX + s))
                for s in range(8):
                    if s == SPLIT:
                        for k in range(MIXK):
                            pool.wait_ge(mixed_hi, layer * MIXK + k + 1)
                            rows = mixed_rows(k)
                            nc.gpsimd.tensor_tensor(act_lo[0:rows, k, :], mixed_tile(k),
                                                    act_hi[0:rows, k, :].bitcast(F32),
                                                    ALU.subtract).then_inc(mixed_split, 1)
                    split(layer, S_MIXOUT + s, s % RAW, slot_width(S_MIXOUT))
                rest(layer, S_KV, 16, 0)
                rest(layer, S_Q, 8, 0)
                rest(layer, S_AO, 8, 0)
                ffn(layer, 1, 3)

        @block.tensor
        def _(pe):
            pe.sem_inc(slot_multiplied, SPLIT)

            def passes(o, a_hi, a_lo, b_hi, b_lo, start, stop):
                nc.tensor.matmul(o, a_hi, b_hi, start=start, stop=False)
                nc.tensor.matmul(o, a_hi, b_lo, start=False, stop=False)
                return nc.tensor.matmul(o, a_lo, b_hi, start=False, stop=stop)

            def weight(r, u, rows=P):
                return (w_hi[0:rows, r, u * P:(u + 1) * P], w_lo[0:rows, r, u * P:(u + 1) * P])

            def act(k, rows=P):
                return act_hi[0:rows, k, :], act_lo[0:rows, k, :]

            def slot_ready(layer, s):
                pe.wait_ge(slot_split, layer * SLOTS + s + (RAW + 1))

            def tile_of(layer, s, o, r, operand, n, start=True, stop=True, rows=lambda k: P):
                pe.wait_ge(w_hi_made, layer * (SLOTS - 2) + s - 1)
                for k in range(n):
                    hi = weight(r, k, rows(k))[0]
                    b_hi, b_lo = operand(k, rows(k))
                    nc.tensor.matmul(o, hi, b_hi, start=start and k == 0, stop=False)
                    nc.tensor.matmul(o, hi, b_lo, start=False, stop=False)
                slot_ready(layer, s)
                for k in range(n):
                    last = nc.tensor.matmul(o, weight(r, k, rows(k))[1], operand(k, rows(k))[0],
                                            start=False, stop=stop and k == n - 1)
                last.then_inc(slot_multiplied, 1)

            def tokens_of(layer, s, n, outs, a_hi, a_lo, width, k0):
                r = s % SPLIT
                pe.wait_ge(w_hi_made, layer * (SLOTS - 2) + s - 1)
                for u in range(n):
                    for t, o in enumerate(outs):
                        for a in (a_hi, a_lo):
                            nc.tensor.matmul(o, a[:, k0 + u, t * P:(t + 1) * P],
                                             w_hi[:, r, u * width:(u + 1) * width],
                                             start=k0 + u == 0 and a is a_hi, stop=False)
                slot_ready(layer, s)
                for u in range(n):
                    for t, o in enumerate(outs):
                        last = nc.tensor.matmul(o, a_hi[:, k0 + u, t * P:(t + 1) * P],
                                                w_lo[:, r, u * width:(u + 1) * width],
                                                start=False, stop=k0 + u == KT - 1)
                last.then_inc(slot_multiplied, 1)

            def first_pair(layer, s, n, rows, hi_arrived, lo_arrived, act=act):
                slot_ready(layer, s)
                slot_ready(layer, s + 1)
                for k in range(n):
                    hi_arrived(k)
                    b_hi, b_lo = act(k, rows(k))
                    for j in range(2):
                        for part in range(2):
                            nc.tensor.matmul(bank(j), weight(j, k, rows(k))[part], b_hi,
                                             start=k == 0 and part == 0, stop=False)
                    lo_arrived(k)
                    for j in range(2):
                        last = nc.tensor.matmul(bank(j), weight(j, k, rows(k))[0], b_lo,
                                                start=False, stop=k == n - 1)
                        if k == n - 1:
                            last.then_inc(slot_multiplied, 1)

            def x_arrived(layer, c):
                return (lambda k: pe.wait_ge(x_hi_made, layer * 4 * KT + c * KT + k + 1),
                        lambda k: pe.wait_ge(x_split, layer * 4 * KT + c * KT + k + 1))

            def stats(layer, n):
                done = layer * 4 * KT + (n + 1) * KT
                pe.wait_ge(consts_loaded, 16)

                def total(a, source, before):
                    for t in range(TT):
                        last = nc.tensor.matmul(psum[:, 6, a * TT + t:a * TT + t + 1],
                                                source[:, t * P:(t + 1) * P], average,
                                                start=before and a == 0 and t == 0,
                                                stop=not before and a == 1 and t == TT - 1)
                    return last

                pe.wait_ge(z_summed, (layer * 4 + n + 1) * (KT - 1) + 2)
                total(0, zsum, True)
                total(1, zsqsum, True)
                pe.wait_ge(z_added, done + 2)
                total(0, x[:, KT - 1, :], False)
                pe.wait_ge(z_squared, done)
                total(1, zsq(KT - 1), False).then_inc(stats_ready, 1)

            def bcast(layer, n):
                pe.wait_ge(ident_made, 1)
                pe.wait_ge(scalars_split, layer * 4 + n + 1)
                for a in range(2):
                    for t in range(TT):
                        for part in range(2):
                            c = 8 * part + TT * a + t
                            last = nc.tensor.matmul(psum[:, 4 + a, t * P:(t + 1) * P],
                                                    small_split[:, c:c + 1].to_broadcast([P, P]),
                                                    ident_r[:, :], start=part == 0,
                                                    stop=part == 1)
                last.then_inc(bcast_ready, 1)

            def ffn(layer, f, c, n):
                base = layer * (2 * FT) + f * FT

                def pair(i, j, p0, first):
                    s = p0
                    pe.wait_ge(gate_silu, base + i + 1)
                    pe.wait_ge(h_made, base + i + 1)
                    if first:
                        first_pair(layer, s, KT, lambda k: P, *x_arrived(layer, c))
                        return
                    for g in range(2):
                        tile_of(layer, s + g, bank(2 * j + g), g, act, KT)

                pair(0, 0, S_IN[f], True)
                pair(1, 1, S_IN[f] + 2, False)
                with pe.Fori(1, FT // 2) as it:
                    for j in range(2):
                        pair(it * 2 + j, j, it * 4 + (S_IN[f] + 2 * j), False)
                with pe.Fori(0, KT // 2) as it:
                    for j in range(2):
                        pe.wait_ge(z_added, layer * 4 * KT + it * 2 + (n * KT + j + 1))
                        for r in range(2):
                            pe.wait_ge(h_split, base + (r + 1) * FT // 2)
                            tile_of(layer, it * 4 + (S_OUT[f] + 2 * j + r), bank(j), r,
                                    lambda u, rows: (h_hi[:, FT // 2 * r + u, :],
                                                     h_lo[:, FT // 2 * r + u, :]),
                                    FT // 2, r == 0, r == 1)
                stats(layer, n)
                bcast(layer, n)

            def out_rest(layer, s0, n, units, rows, act):
                with pe.Fori(1, KT // 2) as it:
                    for j in range(2):
                        pe.wait_ge(z_added, layer * 4 * KT + it * 2 + (n * KT + j + 1))
                        tile_of(layer, it * 2 + (s0 + j), bank(j), j, act, units, rows=rows)

            def mixer(layer):
                E = layer * EVACS

                def project(kind, i):
                    n = [t[0:2] for t in MIX_TILES].index((kind, i))
                    _, _, by_act, by_dve = MIX_TILES[n]
                    if by_act:
                        pe.wait_ge(evac, E + by_act)
                    if by_dve:
                        pe.wait_ge(ca_used, layer * CT + by_dve)
                    s = S_MIX + MIX_SLOT[kind, i]
                    tile_of(layer, s, bank(n % 4), s % SPLIT, act, KT)

                first_pair(layer, S_MIX, KT, lambda k: P, *x_arrived(layer, 1))
                project("xa", 2)
                for i in range(2):
                    project("cg", i)
                for i in range(2):
                    project("ca", i)
                pe.wait_ge(vectors_loaded, layer * 32 + 32)
                for t in range(AT):
                    pe.wait_ge(xc_ready, layer * AT + t + 1)
                    for g in range(2):
                        n = 2 * t + g
                        if n >= 4:
                            pe.wait_ge(rg_gate_read, layer * 6 + n - 3)
                        nc.tensor.matmul(bank(4 + n % 4), mats[:, (AT * g + t) * P:][:, 0:P],
                                         XC[t], start=True, stop=True).then_inc(rg_gate_ready, 1)
                for kind, i in (("k", 0), ("k", 1), ("q", 0), ("g", 0), ("q", 1)):
                    project(kind, i)
                pe.wait_ge(evac, E + EV["g", 0])
                pe.wait_ge(rg_gate_read, layer * 6 + 6)
                for g in range(2):
                    last = nc.tensor.matmul(bank(6 + g),
                                            mats[LR_ROW:LR_ROW + RANK, (2 * AT + g) * P:][:, 0:P],
                                            lr, start=True, stop=True)
                last.then_inc(gla_gate_ready, 1)
                project("g", 1)
                pe.wait_ge(gla_gate_read, layer + 1)
                for s in range(2):
                    tokens_of(layer, S_MIX + V_SLOT + s, 4,
                              [bank(4 + t, P, W_B) for t in range(TT)],
                              act_hi, act_lo, W_B, s * 4)
                project("g", 2)
                pe.wait_ge(evac, E + EV["v", 3])
                pe.wait_ge(gla_qk, layer * 2 + 2)
                for t in range(TT):
                    for g in range(2):
                        last = nc.tensor.transpose(
                            psum[:, 6 + t // 2, (t % 2 * 2 + g) * P:(t % 2 * 2 + g + 1) * P],
                            GP[g][:, t * P:(t + 1) * P], ident)
                last.then_inc(ktok_ready, 1)
                project("g", 3)
                pe.wait_ge(ktok_read, layer + 1)
                for n in range(NCHUNK - 1):
                    if n >= 2:
                        pe.wait_ge(state_ready, layer * (NCHUNK - 1) + n - 1)
                    t, r0 = n // 2, n % 2 * CHUNK
                    for g in range(2):
                        last = nc.tensor.matmul(
                            psum[:, 4 + n % 2, g * 2 * DV:(g + 1) * 2 * DV],
                            k_tok[r0:r0 + CHUNK, t, g * P:(g + 1) * P],
                            v_tok[r0:r0 + CHUNK, t, g * 2 * DV:(g + 1) * 2 * DV],
                            start=True, stop=True)
                    last.then_inc(u_ready, 1)

                def scores(h):
                    if h < 2:
                        pe.wait_ge(state_ready, layer * (NCHUNK - 1) + NCHUNK - 1)
                    else:
                        pe.wait_ge(score_masked, layer * HEADS + h - 1)
                    g, r0 = h // 2, h % 2 * CHUNK
                    for t in range(TT):
                        cols = slice(t * P, (t + 1) * P)
                        last = nc.tensor.matmul(psum[:, 4 + h % 2, cols], KI[g][r0:r0 + CHUNK, cols],
                                                QQ[g][r0:r0 + CHUNK, cols], start=True, stop=True)
                    last.then_inc(score_ready, 1)

                def output(h):
                    pe.wait_ge(score_masked, layer * HEADS + h + 1)
                    if h >= 2:
                        pe.wait_ge(o_read, layer * HEADS + h - 1)
                    g, r0 = h // 2, h % 2 * CHUNK
                    for t in range(TT):
                        nc.tensor.matmul(psum[0:DV, 6 + h % 2, t * P:(t + 1) * P],
                                         v_tok[:, t, h * DV:(h + 1) * DV],
                                         SC[h % 2][:, t * P:(t + 1) * P], start=True, stop=False)
                        for n in (2 * t, 2 * t + 1):
                            if n:
                                cols = slice(n * CHUNK, (n + 1) * CHUNK)
                                last = nc.tensor.matmul(psum[0:DV, 6 + h % 2, cols],
                                                        state[r0:r0 + CHUNK, n, g, :],
                                                        QQ[g][r0:r0 + CHUNK, cols],
                                                        start=False, stop=n % 2 == 1)
                    last.then_inc(o_ready, 1)

                def group_norm(t, source, ready, signal):
                    pe.wait_ge(ready, layer * CT + t + 1)
                    if signal is gn_mean:
                        pe.wait_ge(evac, E + EV["g", 3 - t])
                    nc.tensor.matmul(bank(GN_BANK[t]), block64, source[t],
                                     start=True, stop=True).then_inc(signal, 1)

                def rms(h):
                    pe.wait_ge(o_read, layer * HEADS + h + 1)
                    if h < 2:
                        pe.wait_ge(score_masked, layer * HEADS + 3 + h)
                    else:
                        pe.wait_ge(rms_root, layer * HEADS + h - 1)
                    nc.tensor.matmul(bank(4 + h % 2, DV), ones96, OSQ[h][0:DV, :],
                                     start=True, stop=True).then_inc(rms_ready, 1)

                scores(0)
                scores(1)
                project("ya", 0)
                group_norm(0, CC, conv_done, gn_mean)
                group_norm(1, CC, conv_done, gn_mean)
                output(0)
                scores(2)
                group_norm(0, SQ, gn_squared, gn_var)
                group_norm(1, SQ, gn_squared, gn_var)
                output(1)
                scores(3)
                project("ya", 1)
                rms(0)
                rms(1)
                output(2)
                output(3)
                pe.wait_ge(gn_root, layer * CT + 2)
                project("ya", 2)
                rms(2)
                rms(3)
                first_pair(layer, S_MIXOUT, MIXK, mixed_rows,
                           lambda k: pe.wait_ge(mixed_hi, layer * MIXK + k + 1),
                           lambda k: pe.wait_ge(mixed_split, layer * MIXK + k + 1))
                out_rest(layer, S_MIXOUT, 1, MIXK, mixed_rows, act)

            def attention(layer):
                pe.wait_ge(mem_split, layer + 1)

                def k_tile(m):
                    if m < 2:
                        pe.wait_ge(gn_root, layer * CT + m + 1)
                    else:
                        pe.wait_ge(kv_read, layer * 12 + m - 1)
                    tile_of(layer, S_KV + m, bank(2 + m % 2, P, MEM), m % SPLIT,
                            lambda k, rows: (mem_hi[:, k, :], mem_lo[:, k, :]), KT)

                k_tile(0)
                k_tile(1)
                stats(layer, 1)
                k_tile(2)
                bcast(layer, 1)
                for m in range(3, KT):
                    k_tile(m)
                for half in range(2):
                    if half:
                        pe.wait_ge(kv_read, layer * 12 + 8)
                    else:
                        pe.wait_ge(y_centered, layer * 4 * KT + 2 * KT)
                    for s in range(4):
                        tokens_of(layer, S_KV + 8 + 4 * half + s, 2,
                                  [bank(V_BANK[half] + m) for m in range(2)],
                                  mem_hi, mem_lo, SEQ, s * 2)
                pe.wait_ge(x_split, layer * 4 * KT + 3 * KT)

                def q_tile(m):
                    pe.wait_ge(q_split, layer * KT + m + 1)
                    tile_of(layer, S_Q + m, bank(m % 2), m % SPLIT, act, KT)

                def scores(h):
                    pe.wait_ge(kv_split, layer * 2 + 2)
                    pe.wait_ge(q_split, layer * KT + 2 * h + 2 + 2)
                    if h >= 1:
                        pe.wait_ge(exp_ready, layer * XH + h)
                    for t in range(TT):
                        o = psum[:, 2 + t // 2, t % 2 * MEM:(t % 2 + 1) * MEM]
                        cols = slice(t * P, (t + 1) * P)
                        for u in range(2):
                            k = 2 * h + u
                            last = passes(o, q_hi[:, k, cols], q_lo[:, k, cols],
                                          kT_hi[:, k, :], kT_lo[:, k, :], u == 0, u == 1)
                    last.then_inc(qk_ready, 1)

                def turn(h):
                    pe.wait_ge(probs_ready, layer * XH + h + 1)
                    if h >= 1:
                        pe.wait_ge(pT_split, layer * XH + h)
                    for t in range(TT):
                        for m in range(2):
                            last = nc.tensor.transpose(psum[:, 4 + m, t * P:(t + 1) * P],
                                                       probs[:, h % 2, t, m * P:(m + 1) * P], ident)
                    last.then_inc(pT_ready, 1)

                def context(h):
                    pe.wait_ge(pT_split, layer * XH + h + 1)
                    for e in range(2):
                        if h >= 1:
                            pe.wait_ge(ctx_split, layer * KT + 2 * h - 1 + e)
                        cols = slice((2 * h + e) * P, (2 * h + e + 1) * P)
                        for m in range(2):
                            last = passes(bank(6 + e), v_hi[:, m, cols], v_lo[:, m, cols],
                                          pT_hi[:, m, :], pT_lo[:, m, :], m == 0, m == 1)
                        last.then_inc(ctx_ready, 1)

                for m in range(3):
                    q_tile(m)
                for h in range(XH - 1):
                    scores(h)
                    if h >= 1:
                        context(h - 1)
                    q_tile(2 * h + 3)
                    turn(h)
                    if h < XH - 2:
                        q_tile(2 * h + 4)
                scores(XH - 1)
                context(XH - 2)

                def context_arrived(k):
                    if k == 2:
                        turn(XH - 1)
                    if k == 2 * (XH - 1):
                        context(XH - 1)
                    pe.wait_ge(ctx_hi_made, layer * KT + k + 1)

                def ctx_operand(k, rows=P):
                    return q_hi[0:rows, k, :], q_lo[0:rows, k, :]

                first_pair(layer, S_AO, KT, lambda k: P, context_arrived,
                           lambda k: pe.wait_ge(ctx_split, layer * KT + k + 1), ctx_operand)
                out_rest(layer, S_AO, 2, KT, lambda k: P, ctx_operand)
                stats(layer, 2)
                bcast(layer, 2)

            with pe.Fori(0, LAYERS) as layer:
                ffn(layer, 0, 0, 0)
                mixer(layer)
                attention(layer)
                ffn(layer, 1, 3, 3)

        @block.scalar
        def _(act):
            act.sem_inc(gate_silu, 2)
            A = nc.scalar.activation

            def vec(c, rows=P):
                return vecs[0:rows, c:c + 1]

            for part in range(4):
                act.dma_start(x[:, 2 * part:2 * part + 2, :],
                              x_in[:, 2 * part:2 * part + 2, :]).then_inc(x_loaded[part], 16)
            act.dma_start(consts[:, :], consts_in).then_inc(consts_loaded, 16)
            act.wait_ge(eps_set, 1)
            A(small[:, 46:47], small[:, 47:48], ACT.Silu)
            for k in range(KT):
                act.wait_ge(x_loaded[k // 2], 16)
                A(act_hi[:, k, :], x[:, k, :], ACT.Copy).then_inc(x_hi_made, 1)
            act.wait_ge(consts_loaded, 16)
            A(ident_r[:, :], ident, ACT.Copy).then_inc(ident_made, 1)

            def advance(layer, s, place, rnd, width):
                act.wait_ge(slot_multiplied, layer * SLOTS + s + (SPLIT + 1))
                if width:
                    act.wait_ge(raw_loaded[place], (layer * (SLOTS // RAW) + rnd + 1) * 16)
                    A(w_hi[:, place % SPLIT, 0:width], raw[:, place, 0:width],
                      ACT.Copy).then_inc(w_hi_made, 1)

            def step(layer, s):
                n = s + SPLIT
                advance(layer, s, n % RAW, n // RAW, slot_width(n) if n < SLOTS else 0)

            def rounds(layer, s0, n, body, between=None, first=None):
                def adv(it, last):
                    def f(j):
                        m = j + SPLIT
                        if last:
                            step(layer, s0 + it * RAW + j)
                        else:
                            advance(layer, it * RAW + (s0 + j), m % RAW,
                                    it + (s0 // RAW + m // RAW), slot_width(s0))
                    return f
                if first:
                    body(0, adv(0, True), first)
                with act.Fori(1 if first else 0, n // RAW - 1) as it:
                    body(it, adv(it, False))
                if between:
                    between()
                body(n // RAW - 1, adv(n // RAW - 1, True))

            def squares(layer, n, s0, per_tile, between=None):
                A(small[:, 46:47], small[:, 47:48], ACT.Sqrt)

                def body(it, adv):
                    for j in range(RAW // per_tile):
                        for r in range(per_tile):
                            adv(j * per_tile + r)
                        m = it * (RAW // per_tile) + j
                        z = layer * 4 * KT + m + n * KT
                        act.wait_ge(z_added, z + (2 + 1))
                        act.wait_ge(z_summed, layer * 4 * (KT - 1) + m + (n * (KT - 1) + 1))
                        A(zsq(j), x[:, bass.ds(m, 1), :].rearrange("p a s -> p (a s)"),
                          ACT.Square).then_inc(z_squared, 1)
                rounds(layer, s0, KT * per_tile, body, between)

            def root(layer, n):
                act.wait_ge(var_ready, layer * 4 + n + 1)
                A(small[:, 16:20], small[:, 12:16], ACT.Sqrt).then_inc(std_ready, 1)
                if n >= 2:
                    A(small[:, 46:47], small[:, 47:48], ACT.Silu)

            def affine(layer, n, k):
                act.wait_ge(y_centered, layer * 4 * KT + n * KT + k + 1)
                c = V_LN + 16 * n + k
                A(x[:, k, :], x[:, k, :], ACT.Identity, bias=vec(c + 8), scale=vec(c))
                act.drain()
                A(act_hi[:, k, :], x[:, k, :], ACT.Copy).then_inc(x_hi_made, 1)

            def ffn(layer, f, n):
                base = layer * (2 * FT) + f * FT

                def body(it, adv, first=None):
                    for j in range(2):
                        adv(2 * j)
                        act.wait_ge(h_made, base + it * 2 + (j + 1))
                        A(work[:, j, :], bank(2 * j), ACT.Silu).then_inc(gate_silu, 1)
                        adv(2 * j + 1)
                        if first:
                            first(layer, j)
                rounds(layer, S_IN[f], 2 * FT, body, first=decay_rates if f == 0 else None)
                squares(layer, n, S_OUT[f], 2)
                root(layer, n)
                for k in range(KT):
                    affine(layer, n, k)

            def decay_rates(layer, part):
                lm = vecs[:, V_LAM:V_LAM + AT]

                def l(n):
                    return lam[:, n * AT:(n + 1) * AT]

                if part == 0:
                    act.wait_ge(vectors_loaded, layer * 32 + 32)
                    A(l(0), lm, ACT.Abs)
                    act.drain()
                    A(l(1), l(0), ACT.Exp, scale=-1.0)
                    act.drain()
                    A(l(2), l(1), ACT.Ln, bias=1.0).then_inc(lam_log, 1)
                else:
                    act.drain()
                    A(l(3), l(2), ACT.Tanh, scale=0.5).then_inc(lam_tanh, 1)
                A(small[:, 46:47], small[:, 47:48], ACT.Silu)

            def mixer(layer):
                def read(kind, i):
                    step(layer, S_MIX + MIX_SLOT[kind, i])
                    return bank([t[0:2] for t in MIX_TILES].index((kind, i)) % 4)

                def l(n):
                    return lam[:, n * AT:(n + 1) * AT]

                for t in range(AT):
                    A(xa_pad[:, t, RG_K - 1:], read("xa", t), ACT.Copy).then_inc(evac, 1)
                for t in range(CT):
                    A(CC[t], read("cg", t), ACT.Sigmoid).then_inc(evac, 1)
                for t in range(CT):
                    step(layer, S_MIX + MIX_SLOT["ca", t])
                for t in range(AT):
                    for g, (dst, c) in enumerate(((RR, V_BR), (II, V_BI))):
                        n = 2 * t + g
                        act.wait_ge(rg_gate_ready, layer * 6 + n + 1)
                        A(dst[t], bank(4 + n % 4), ACT.Sigmoid, bias=vec(c + t)).then_inc(
                            rg_gate_read, 1)
                act.drain()
                act.wait_ge(lam_ready, layer + 1)
                for t in range(AT):
                    A(TH[t], RR[t], ACT.Tanh, scale=l(11)[:, t:t + 1])
                A(KK[0], read("k", 0), ACT.Copy).then_inc(evac, 1)
                for t in range(AT):
                    A(EE[t], RR[t], ACT.Exp, scale=l(12)[:, t:t + 1])
                act.drain()
                A(KK[1], read("k", 1), ACT.Copy).then_inc(evac, 1)
                for t in range(AT):
                    A(RR[t], TH[t], ACT.Sqrt).then_inc(rg_factors, 1)
                A(QQ[0], read("q", 0), ACT.Copy).then_inc(evac, 1)
                b = read("g", 0)
                A(lr, b[LR_ROW:LR_ROW + RANK, :], ACT.Copy)
                A(GG[0][0:DV, :], b[0:DV, :], ACT.Silu).then_inc(evac, 1)
                A(QQ[1], read("q", 1), ACT.Copy).then_inc(evac, 1)
                act.wait_ge(gla_gate_ready, layer + 1)
                for g in range(2):
                    A(GP[g], bank(6 + g), ACT.Identity, bias=vec(V_BG + g))
                    last = A(CU[g], bank(6 + g), ACT.Abs, bias=vec(V_BG + g))
                last.then_inc(gla_gate_read, 1)
                act.drain()
                for g in range(2):
                    A(CU[g], CU[g], ACT.Exp, scale=-1.0)
                act.drain()
                for g in range(2):
                    A(CU[g], CU[g], ACT.Ln, bias=1.0).then_inc(gla_log, 1)
                A(GG[1][0:DV, :], read("g", 1)[0:DV, :], ACT.Silu).then_inc(evac, 1)
                for g in range(2):
                    act.wait_ge(gla_cum, layer * 2 + g + 1)
                    A(EB[g], CU[g], ACT.Exp, scale=1 / 16)
                    A(KI[g], CU[g], ACT.Exp, scale=-1 / 16)
                    A(GP[g], GP[g], ACT.Exp, scale=1 / 16).then_inc(gla_exp, 1)
                for s in range(2):
                    step(layer, S_MIX + V_SLOT + s)
                for t in range(TT):
                    A(v_tok[:, t, :], bank(4 + t, P, W_B), ACT.Copy).then_inc(evac, 1)
                act.wait_ge(gla_qk, layer * 2 + 2)
                A(GG[2][0:DV, :], read("g", 2)[0:DV, :], ACT.Silu).then_inc(evac, 1)
                act.wait_ge(ktok_ready, layer + 1)
                A(k_tok[:, 0:2, :].rearrange("p t e -> p (t e)"), bank(6), ACT.Copy)
                A(k_tok[:, 2:4, :].rearrange("p t e -> p (t e)"), bank(7), ACT.Copy).then_inc(
                    ktok_read, 1)
                A(GG[3][0:DV, :], read("g", 3)[0:DV, :], ACT.Silu).then_inc(evac, 1)

                def gelu(t):
                    A(YA[t], read("ya", t), ACT.Gelu_apprx_tanh).then_inc(evac, 1)

                def read_o(h):
                    act.wait_ge(o_ready, layer * HEADS + h + 1)
                    A(OO[h][0:DV, :], bank(6 + h % 2, DV), ACT.Copy)
                    A(OSQ[h][0:DV, :], bank(6 + h % 2, DV), ACT.Square).then_inc(o_read, 1)

                def rms_sqrt(h):
                    act.wait_ge(rms_ready, layer * HEADS + h + 1)
                    if h >= 2:
                        act.wait_ge(head_mixed, layer * HEADS + h - 1)
                    A(RS[h % 2][0:DV, :], bank(4 + h % 2, DV), ACT.Sqrt,
                      bias=small[0:DV, 47:48]).then_inc(rms_root, 1)

                def hi(k):
                    kind, i = MIX_ORDER[k]
                    if kind == "r":
                        act.wait_ge(rg_mixed, layer * AT + i + 1)
                    if kind == "h":
                        act.wait_ge(head_mixed, layer * HEADS + i + 1)
                    A(act_hi[0:mixed_rows(k), k, :], mixed_tile(k), ACT.Copy).then_inc(mixed_hi, 1)

                act.wait_ge(rg_scanned, layer * AT + AT)
                gelu(0)
                for t in range(CT):
                    act.wait_ge(gn_centered, layer * CT + t + 1)
                    A(SQ[t], CC[t], ACT.Square).then_inc(gn_squared, 1)
                read_o(0)
                for t in range(CT):
                    act.wait_ge(gn_var, layer * CT + t + 1)
                    A(SQ[t], bank(GN_BANK[t]), ACT.Sqrt, bias=small[:, 47:48]).then_inc(gn_root, 1)
                read_o(1)
                gelu(1)
                rms_sqrt(0)
                rms_sqrt(1)
                read_o(2)
                read_o(3)
                for t in range(CT):
                    act.wait_ge(gn_scaled, layer * CT + t + 1)
                    A(CC[t], CC[t], ACT.Silu, scale=vec(V_GG + t), bias=vec(V_GB + t))
                gelu(2)
                act.drain()
                for k in range(4):
                    hi(k)
                rms_sqrt(2)
                rms_sqrt(3)
                for k in range(4, MIXK):
                    hi(k)

                def split_mem():
                    act.wait_ge(mem_loaded, layer * 16 + 16)
                    A(mem_hi[:, :, :], mem_raw[:, :, :], ACT.Copy).then_inc(mem_hi_made, 1)

                squares(layer, 1, S_MIXOUT, 1, split_mem)

            def attention(layer):
                def read_k(m):
                    step(layer, S_KV + m)
                    A(k_st[:, m, :], bank(2 + m % 2, P, MEM), ACT.Copy).then_inc(kv_read, 1)

                read_k(0)
                read_k(1)
                root(layer, 1)
                read_k(2)
                for k in range(KT):
                    affine(layer, 1, k)
                    if k % 2 == 1 and k // 2 < 4:
                        read_k(3 + k // 2)
                read_k(7)
                for half in range(2):
                    for s in range(4):
                        step(layer, S_KV + 8 + 4 * half + s)
                    for m in range(2):
                        A(v_st[:, m, half * SEQ:(half + 1) * SEQ], bank(V_BANK[half] + m),
                          ACT.Copy).then_inc(kv_read, 1)
                act.wait_ge(kv_split, layer * 2 + 2)

                def q_tile(m):
                    step(layer, S_Q + m)
                    A(q_hi[:, m, :], bank(m % 2), ACT.Copy).then_inc(q_hi_made, 1)

                def exps(h):
                    act.wait_ge(max_ready, layer * XH + h + 1)
                    if h >= 2:
                        act.wait_ge(pT_ready, layer * XH + h - 1)
                    for t in range(TT):
                        last = A(probs[:, h % 2, t, :],
                                 psum[:, 2 + t // 2, t % 2 * MEM:(t % 2 + 1) * MEM],
                                 ACT.Exp, scale=XSCALE,
                                 bias=small[:, 24 + h % 2 * 4 + t:25 + h % 2 * 4 + t],
                                 accum_out=small[:, 32 + h % 2 * 4 + t:33 + h % 2 * 4 + t])
                    last.then_inc(exp_ready, 1)

                def turned(h):
                    act.wait_ge(pT_ready, layer * XH + h + 1)
                    if h >= 1:
                        act.wait_ge(ctx_ready, layer * KT + 2 * h)
                    A(pT_hi[:, :, :], psum[:, 4:6, :], ACT.Copy).then_inc(pT_hi_made, 1)

                def context(h):
                    for e in range(2):
                        act.wait_ge(ctx_ready, layer * KT + 2 * h + e + 1)
                        A(q_hi[:, 2 * h + e, :], bank(6 + e), ACT.Copy).then_inc(ctx_hi_made, 1)

                for m in range(3):
                    q_tile(m)
                for h in range(XH - 1):
                    exps(h)
                    if h >= 1:
                        context(h - 1)
                    q_tile(2 * h + 3)
                    turned(h)
                    if h < XH - 2:
                        q_tile(2 * h + 4)
                exps(XH - 1)
                context(XH - 2)
                turned(XH - 1)
                context(XH - 1)
                squares(layer, 2, S_AO, 1)
                root(layer, 2)
                for k in range(KT):
                    affine(layer, 2, k)

            with act.Fori(0, LAYERS) as layer:
                act.drain()
                act.dma_start(vecs[:, :], vecs_in[bass.ds(layer, 1)].rearrange(
                    "a p n -> (a p) n")).then_inc(vectors_loaded, 16)
                act.dma_start(mats[:, :], mats_in[bass.ds(layer, 1)].rearrange(
                    "a p n -> (a p) n")).then_inc(vectors_loaded, 16)
                ffn(layer, 0, 0)
                mixer(layer)
                attention(layer)
                ffn(layer, 1, 3)

        @block.vector
        def _(dve):
            V = nc.vector
            dve.sem_inc(h_made, 2)
            dve.sem_inc(z_added, 2)
            dve.sem_inc(z_summed, 2)
            dve.sem_inc(q_split, 2)
            V.memset(small[:, 47:48], EPS).then_inc(eps_set, 1)
            dve.wait_ge(consts_loaded, 16)
            for part in range(4):
                dve.wait_ge(x_loaded[part], 16)

            def vec(c, rows=P):
                return vecs[0:rows, c:c + 1]

            def done(layer, s):
                dve.wait_ge(slot_multiplied, layer * SLOTS + s + (SPLIT + 1))

            def xt(it, j):
                return x[:, bass.ds(it * 2 + j, 1), :].rearrange("p a s -> p (a s)")

            def residual(layer, n, s0, per_tile, alpha, between=None):
                dve.drain()
                V.memset(work[:, 0:2, :], 0.0)

                def tiles(it, last=False):
                    for j in range(2):
                        z = layer * 4 * KT + it * 2 + (n * KT + j)
                        done(layer, it * (2 * per_tile) + (s0 + (j + 1) * per_tile - 1))
                        V.scalar_tensor_tensor(xt(it, j), xt(it, j), alpha, bank(j), ALU.mult,
                                               ALU.add).then_inc(z_added, 1)
                        if last and j == 1:
                            return
                        dve.drain()
                        V.tensor_tensor(zsum, zsum, xt(it, j), ALU.add)
                        dve.wait_ge(z_squared, z + 1)
                        V.tensor_tensor(zsqsum, zsqsum, zsq(j), ALU.add).then_inc(z_summed, 1)

                if between:
                    with dve.Fori(0, KT // 4) as it:
                        tiles(it)
                    between()
                with dve.Fori(KT // 4 if between else 0, KT // 2 - 1) as it:
                    tiles(it)
                tiles(KT // 2 - 1, True)

            def norm(layer, n, eps):
                dve.wait_ge(stats_ready, layer * 4 + n + 1)
                V.tensor_copy(small[:, 0:4], psum[:, 6, 0:4])
                dve.drain()
                V.tensor_tensor(small[:, 8:12], small[:, 0:4], small[:, 0:4], ALU.mult)
                dve.drain()
                V.tensor_tensor(small[:, 8:12], psum[:, 6, 4:8], small[:, 8:12], ALU.subtract)
                dve.drain()
                V.tensor_scalar(small[:, 12:16], small[:, 8:12], 0.0, eps, ALU.max,
                                ALU.add).then_inc(var_ready, 1)
                dve.wait_ge(std_ready, layer * 4 + n + 1)
                V.reciprocal(small[:, 8:12], small[:, 16:20])
                dve.drain()
                V.tensor_tensor(small[:, 8:12], small[:, 8:12], small[:, 12:16], ALU.mult)
                dve.drain()
                V.tensor_tensor(small[:, 8:12], small[:, 8:12], small[:, 16:20], ALU.add)
                dve.drain()
                V.reciprocal(small[:, 16:20], small[:, 8:12])
                dve.drain()
                V.tensor_tensor(small[:, 20:24], small[:, 0:4], small[:, 16:20], ALU.mult)
                dve.drain()
                V.tensor_scalar(small_split[:, 0:8], small[:, 16:24], 2.0, None, ALU.mult)
                dve.drain()
                V.scalar_tensor_tensor(small_split[:, 8:16], small[:, 16:24], 2.0,
                                       small_split[:, 0:8].bitcast(F32), ALU.mult,
                                       ALU.subtract).then_inc(scalars_split, 1)
                dve.wait_ge(bcast_ready, layer * 4 + n + 1)
                for k in range(KT):
                    V.tensor_tensor(x[:, k, :], x[:, k, :], bank(4), ALU.mult)
                    dve.drain()
                    V.tensor_tensor(x[:, k, :], x[:, k, :], bank(5),
                                    ALU.subtract).then_inc(y_centered, 1)

            def ffn(layer, f, n):
                base = layer * (2 * FT) + f * FT
                with dve.Fori(0, FT // 2) as it:
                    for j in range(2):
                        i = it * 2 + j
                        h = work[:, 2 + j, :]
                        hi = h_hi[:, bass.ds(i, 1), :].rearrange("p a s -> p (a s)")
                        lo = h_lo[:, bass.ds(i, 1), :].rearrange("p a s -> p (a s)")
                        done(layer, it * 4 + (S_IN[f] + 2 * j + 1))
                        dve.wait_ge(gate_silu, base + i + (2 + 1))
                        V.tensor_tensor(h, work[:, j, :], bank(2 * j + 1),
                                        ALU.mult).then_inc(h_made, 1)
                        dve.drain()
                        V.tensor_copy(hi, h)
                        dve.drain()
                        V.tensor_tensor(lo, h, hi.bitcast(F32), ALU.subtract).then_inc(h_split, 1)
                if f == 0:
                    decay_rates(layer)
                residual(layer, n, S_OUT[f], 2, 2 * ALPHA)
                norm(layer, n, 4 * EPS)

            def decay_rates(layer):
                def l(n):
                    return lam[:, n * AT:(n + 1) * AT]

                dve.wait_ge(lam_log, layer + 1)
                V.tensor_scalar(l(4), l(1), 2.0, None, ALU.add)
                dve.drain()
                V.reciprocal(l(5), l(4))
                dve.drain()
                V.tensor_tensor(l(6), l(1), l(5), ALU.mult)
                V.tensor_scalar(l(10), vecs[:, V_LAM:V_LAM + AT], -1.0, 0.0, ALU.mult, ALU.max)
                dve.wait_ge(lam_tanh, layer + 1)
                V.tensor_tensor(l(7), l(3), l(3), ALU.mult)
                dve.drain()
                V.tensor_tensor(l(8), l(6), l(3), ALU.subtract)
                V.tensor_scalar(l(7), l(7), -1.0, 1.0, ALU.mult, ALU.add)
                dve.drain()
                V.reciprocal(l(9), l(7))
                dve.drain()
                V.tensor_tensor(l(9), l(9), l(8), ALU.mult)
                dve.drain()
                V.scalar_tensor_tensor(l(9), l(9), 2.0, l(2), ALU.mult, ALU.add)
                dve.drain()
                V.tensor_tensor(l(9), l(9), l(10), ALU.add)
                dve.drain()
                V.tensor_scalar(l(11), l(9), 4.0, None, ALU.mult)
                V.tensor_scalar(l(12), l(9), -8.0, None, ALU.mult).then_inc(lam_ready, 1)

            def mixer(layer):
                E = layer * EVACS
                dve.wait_ge(vectors_loaded, layer * 32 + 32)
                V.memset(xa_pad[:, :, 0:RG_K - 1], 0.0)
                V.memset(u_pad[:, :, 0:CONV_K - 1], 0.0)
                for t in range(AT):
                    dve.wait_ge(evac, E + EV["xa", t])
                    V.tensor_scalar(XC[t], xa_pad[:, t, RG_K - 1:],
                                    vec(V_CW + (RG_K - 1) * AT + t), vec(V_CB + t),
                                    ALU.mult, ALU.add)
                    for j in range(RG_K - 1):
                        dve.drain()
                        last = V.scalar_tensor_tensor(XC[t], xa_pad[:, t, j:j + SEQ],
                                                      vec(V_CW + j * AT + t), XC[t],
                                                      ALU.mult, ALU.add)
                    last.then_inc(xc_ready, 1)
                for t in range(CT):
                    done(layer, S_MIX + MIX_SLOT["ca", t])
                    dve.wait_ge(evac, E + EV["cg", t])
                    b = [m[0:2] for m in MIX_TILES].index(("ca", t)) % 4
                    V.tensor_tensor(u_pad[:, t, CONV_K - 1:], CC[t], bank(b),
                                    ALU.mult).then_inc(ca_used, 1)

                def taps(t, j0, j1):
                    for j in range(j0, j1):
                        dve.drain()
                        w = vec(V_DW + j * CT + t)
                        if j == 0:
                            last = V.tensor_scalar(CC[t], u_pad[:, t, 0:SEQ], w, vec(V_DB + t),
                                                   ALU.mult, ALU.add)
                        else:
                            last = V.scalar_tensor_tensor(CC[t], u_pad[:, t, j:j + SEQ], w, CC[t],
                                                          ALU.mult, ALU.add)
                    if j1 == CONV_K:
                        last.then_inc(conv_done, 1)

                taps(0, 0, CONV_K)
                for t in range(AT):
                    dve.wait_ge(rg_factors, layer * AT + t + 1)
                    V.scalar_tensor_tensor(TH[t], EE[t], 1.0, TH[t], ALU.add, ALU.mult)
                    V.scalar_tensor_tensor(RR[t], EE[t], 1.0, RR[t], ALU.add, ALU.mult)
                    V.tensor_tensor(II[t], II[t], XC[t], ALU.mult)
                    dve.drain()
                    V.tensor_scalar(TH[t], TH[t], -1.0, 1.0, ALU.mult, ALU.add)
                    V.tensor_tensor(RR[t], RR[t], II[t], ALU.mult)
                    dve.drain()
                    V.tensor_tensor_scan(XC[t], TH[t], RR[t], 0.0, ALU.mult,
                                         ALU.add).then_inc(rg_scanned, 1)
                taps(1, 0, 12)
                for g in range(2):
                    dve.wait_ge(gla_log, layer * 2 + g + 1)
                    V.scalar_tensor_tensor(GP[g], GP[g], 0.0, CU[g], ALU.min, ALU.subtract)
                    dve.drain()
                    V.tensor_tensor_scan(CU[g], not_start, GP[g], 0.0, ALU.mult, ALU.add)
                    dve.drain()
                    c = CU[g].rearrange("p (n c) -> p n c", c=CHUNK)
                    V.tensor_tensor(GP[g].rearrange("p (n c) -> p n c", c=CHUNK),
                                    c[:, :, CHUNK - 1:CHUNK].to_broadcast([P, NCHUNK, CHUNK]), c,
                                    ALU.subtract).then_inc(gla_cum, 1)
                taps(1, 12, 16)
                dve.wait_ge(evac, E + EV["q", 1])
                V.memset(tmp[:, 37 * SEQ:39 * SEQ], 0.0)
                for g in range(2):
                    dve.wait_ge(gla_exp, layer * 2 + g + 1)
                    V.scalar_tensor_tensor(QQ[g], QQ[g], DK ** -0.5, EB[g], ALU.mult, ALU.mult)
                    V.tensor_tensor(KI[g], KK[g], KI[g], ALU.mult)
                    V.tensor_tensor(GP[g], KK[g], GP[g], ALU.mult).then_inc(gla_qk, 1)
                taps(1, 16, 22)
                for n in range(NCHUNK - 1):
                    dve.drain()
                    dve.wait_ge(u_ready, layer * (NCHUNK - 1) + n + 1)
                    for g in range(2):
                        for r in range(2):
                            rows = slice(r * CHUNK, (r + 1) * CHUNK)
                            c = (2 * g + r) * DV
                            u = psum[rows, 4 + n % 2, c:c + DV]
                            if n == 0:
                                last = V.tensor_copy(state[rows, 1, g, :], u)
                            else:
                                e = (n + 1) * CHUNK - 1
                                last = V.scalar_tensor_tensor(
                                    state[rows, n + 1, g, :], state[rows, n, g, :],
                                    EB[g][rows, e:e + 1], u, ALU.mult, ALU.add)
                    last.then_inc(state_ready, 1)
                taps(1, 22, CONV_K)

                def mask(h):
                    dve.wait_ge(score_ready, layer * HEADS + h + 1)
                    if h >= 2:
                        dve.wait_ge(o_ready, layer * HEADS + h - 1)
                    dve.sem_inc(dve_wait_carrier, 1)
                    m = score_mask.rearrange("p (a c) -> p a c", a=1).to_broadcast([P, TT, P])
                    V.copy_predicated(SC[h % 2].rearrange("p (t c) -> p t c", c=P), m,
                                      bank(4 + h % 2).rearrange("p (t c) -> p t c", c=P)
                                      ).then_inc(score_masked, 1)

                def head(h):
                    rs, o = RS[h % 2][0:DV, :], OO[h][0:DV, :]
                    dve.wait_ge(rms_root, layer * HEADS + h + 1)
                    V.reciprocal(rs, rs)
                    dve.drain()
                    V.scalar_tensor_tensor(o, o, vec(V_NG, DV), rs, ALU.mult, ALU.mult)
                    dve.drain()
                    V.tensor_tensor(o, o, GG[h][0:DV, :], ALU.mult).then_inc(head_mixed, 1)

                def recurrent(t):
                    dve.wait_ge(evac, E + EV["ya", t])
                    V.tensor_tensor(XC[t], XC[t], YA[t], ALU.mult).then_inc(rg_mixed, 1)

                mask(0)
                mask(1)
                for t in range(CT):
                    dve.wait_ge(gn_mean, layer * CT + t + 1)
                    V.tensor_tensor(CC[t], CC[t], bank(GN_BANK[t]), ALU.subtract).then_inc(
                        gn_centered, 1)
                for t in range(CT):
                    mask(2 + t)
                    dve.wait_ge(gn_root, layer * CT + t + 1)
                    V.reciprocal(SQ[t], SQ[t])
                    dve.drain()
                    V.tensor_tensor(CC[t], CC[t], SQ[t], ALU.mult).then_inc(gn_scaled, 1)
                recurrent(0)
                recurrent(1)
                head(0)
                head(1)
                recurrent(2)
                head(2)
                head(3)

                def split_mem():
                    dve.wait_ge(mem_hi_made, layer + 1)
                    V.tensor_tensor(mem_lo[:, :, :], mem_raw[:, :, :],
                                    mem_hi[:, :, :].bitcast(F32),
                                    ALU.subtract).then_inc(mem_split, 1)

                residual(layer, 1, S_MIXOUT, 1, ALPHA, split_mem)

            def attention(layer):
                norm(layer, 1, EPS)
                for k in range(KT):
                    dve.wait_ge(x_hi_made, layer * 4 * KT + 2 * KT + k + 1)
                    V.tensor_tensor(act_lo[:, k, :], x[:, k, :], act_hi[:, k, :].bitcast(F32),
                                    ALU.subtract).then_inc(x_split, 1)
                for n, (st, hi, lo) in enumerate(((k_st, kT_hi, kT_lo), (v_st, v_hi, v_lo))):
                    dve.wait_ge(kv_read, layer * 12 + (8, 12)[n])
                    V.tensor_copy(hi[:, :, :], st[:, :, :])
                    dve.drain()
                    V.tensor_tensor(lo[:, :, :], st[:, :, :], hi[:, :, :].bitcast(F32),
                                    ALU.subtract).then_inc(kv_split, 1)

                def q_tile(m):
                    dve.wait_ge(q_hi_made, layer * KT + m + 1)
                    V.tensor_tensor(q_lo[:, m, :], bank(m % 2), q_hi[:, m, :].bitcast(F32),
                                    ALU.subtract).then_inc(q_split, 1)

                def softmax(h):
                    dve.wait_ge(qk_ready, layer * XH + h + 1)
                    c = 24 + h % 2 * 4
                    V.reduce_max(small[:, 40:44], psum[:, 2:4, :].rearrange(
                        "p a (t m) -> p (a t) m", m=MEM), AX.X)
                    dve.drain()
                    V.tensor_scalar(small[:, c:c + 4], small[:, 40:44], -XSCALE, None,
                                    ALU.mult).then_inc(max_ready, 1)
                    c = 32 + h % 2 * 4
                    dve.wait_ge(exp_ready, layer * XH + h + 1)
                    V.reciprocal(small[:, c:c + 4], small[:, c:c + 4])
                    dve.drain()
                    for t in range(TT):
                        last = V.tensor_scalar(probs[:, h % 2, t, :], probs[:, h % 2, t, :],
                                               small[:, c + t:c + t + 1], None, ALU.mult)
                    last.then_inc(probs_ready, 1)

                def turned(h):
                    dve.wait_ge(pT_hi_made, layer * XH + h + 1)
                    V.tensor_tensor(pT_lo[:, :, :], psum[:, 4:6, :], pT_hi[:, :, :].bitcast(F32),
                                    ALU.subtract).then_inc(pT_split, 1)

                def context(h):
                    for e in range(2):
                        dve.wait_ge(ctx_hi_made, layer * KT + 2 * h + e + 1)
                        V.tensor_tensor(q_lo[:, 2 * h + e, :], bank(6 + e),
                                        q_hi[:, 2 * h + e, :].bitcast(F32),
                                        ALU.subtract).then_inc(ctx_split, 1)

                for m in range(3):
                    q_tile(m)
                for h in range(XH - 1):
                    softmax(h)
                    if h >= 1:
                        context(h - 1)
                    q_tile(2 * h + 3)
                    turned(h)
                    if h < XH - 2:
                        q_tile(2 * h + 4)
                softmax(XH - 1)
                context(XH - 2)
                turned(XH - 1)
                context(XH - 1)
                residual(layer, 2, S_AO, 1, ALPHA)
                norm(layer, 2, EPS)

            with dve.Fori(0, LAYERS) as layer:
                ffn(layer, 0, 0)
                mixer(layer)
                attention(layer)
                ffn(layer, 1, 3)


def kernel(**inputs):
    import numpy as np
    import concourse.bacc as bacc
    from concourse.bass_utils import run_bass_kernel_spmd as run

    a = {k: np.asarray(v) for k, v in inputs.items()}
    L = LAYERS
    f32 = np.float32

    def tiles(w, kt=KT):
        n = w.shape[2] // P
        return np.ascontiguousarray(
            w.reshape(L, kt, P, n, P).transpose(0, 3, 2, 1, 4)).reshape(L * n, P, kt * P)

    def ffn_in(w):
        w = w.reshape(L, KT, P, 2, FT, P).transpose(0, 4, 3, 2, 1, 5)
        return np.ascontiguousarray(w).reshape(L * 2 * FT, P, KT * P)

    def ffn_out(w):
        w = w.reshape(L, 2, FT // 2, P, KT, P).transpose(0, 4, 1, 3, 2, 5)
        return np.ascontiguousarray(w).reshape(L * 2 * KT, P, FT // 2 * P)

    m = a["mix_w_in"]
    xa, ya = m[:, :, 0:384], m[:, :, 384:768]
    q, k = m[:, :, 768:960], m[:, :, 960:1152]
    v, g, lrw = m[:, :, 1152:1536], m[:, :, 1536:1920], m[:, :, 1920:1936]
    ca, cg = m[:, :, 1936:2192], m[:, :, 2192:2448]

    def pairs(w):
        o = np.zeros(w.shape[:-1] + (2 * P,), f32)
        for h in range(HEADS):
            o[..., h * CHUNK:h * CHUNK + DK] = w[..., h * DK:(h + 1) * DK]
        return o

    gg = np.zeros((L, D, HEADS * P), f32)
    for h in range(HEADS):
        gg[:, :, h * P:h * P + DV] = g[:, :, h * DV:(h + 1) * DV]
    gg[:, :, LR_ROW:LR_ROW + RANK] = lrw
    parts = {"xa": xa, "ya": ya, "k": pairs(k), "q": pairs(q), "g": gg, "ca": ca, "cg": cg}
    w_mix = tiles(np.concatenate([parts[n][:, :, i * P:(i + 1) * P] for n, i, _, _ in MIX_TILES], 2))
    w_v = np.ascontiguousarray(v.reshape(L, 2, 4, P, W_B).transpose(0, 1, 3, 2, 4)).reshape(
        L * 2, P, 4 * W_B)
    mo = np.zeros((L, MIXK * P, D), f32)
    src = a["mix_w_out"]
    for n, (kind, i) in enumerate(MIX_ORDER):
        rows, at = {"r": (P, i * P), "h": (DV, W_A + i * DV), "c": (P, W_A + W_B + i * P)}[kind]
        mo[:, n * P:n * P + rows] = src[:, at:at + rows]
    kv = a["xa_w_kv"]
    w_vm = kv[:, :, D:].reshape(L, 4, 2, P, 2, SEQ).transpose(0, 4, 1, 3, 2, 5).reshape(
        L, 8, P, 8 * P)
    w_kv = np.concatenate([tiles(kv[:, :, 0:D]).reshape(L, 8, P, 8 * P), w_vm], 1).reshape(
        L * 16, P, 8 * P)

    def cols(w, n):
        return w.reshape(L, n, P).transpose(0, 2, 1)

    vecs = np.zeros((L, P, NV), f32)
    for s in range(4):
        vecs[:, :, V_LN + 16 * s:V_LN + 16 * s + 8] = cols(a[f"ln{s + 1}_g"], KT)
        vecs[:, :, V_LN + 16 * s + 8:V_LN + 16 * s + 16] = cols(a[f"ln{s + 1}_b"], KT)
    for j in range(RG_K):
        vecs[:, :, V_CW + j * AT:V_CW + (j + 1) * AT] = cols(a["rg_conv_w"][:, j], AT)
    for c, n in ((V_CB, "rg_conv_b"), (V_BR, "rg_b_r"), (V_BI, "rg_b_i"), (V_LAM, "rg_lambda")):
        vecs[:, :, c:c + AT] = cols(a[n], AT)
    vecs[:, :, V_BG:V_BG + 2] = cols(pairs(a["gla_b_gate"]), 2)
    vecs[:, 0:DV, V_NG] = a["gla_norm_g"]
    for j in range(CONV_K):
        vecs[:, :, V_DW + j * CT:V_DW + (j + 1) * CT] = cols(a["cv_dw_w"][:, j], CT)
    for c, n in ((V_DB, "cv_dw_b"), (V_GG, "cv_gn_g"), (V_GB, "cv_gn_b")):
        vecs[:, :, c:c + CT] = cols(a[n], CT)
    mats = np.zeros((L, P, 1024), f32)
    for g_, n in enumerate(("rg_w_r", "rg_w_i")):
        for b in range(W_A // 64):
            r = b % 2 * 64
            c = (AT * g_ + b // 2) * P + r
            mats[:, r:r + 64, c:c + 64] = a[n][:, b]
    mats[:, LR_ROW:LR_ROW + RANK, 2 * AT * P:] = pairs(a["gla_w_gate"])

    consts = np.zeros((P, NC_), f32)
    idx = np.arange(P)
    consts[:, C_ID:C_ID + P] = np.eye(P, dtype=f32)
    consts[:, C_ONE:C_ONE + P] = 1.0
    same = idx[:, None] // 64 == idx[None, :] // 64
    consts[:, C_B64:C_B64 + P] = np.where(same, f32(1 / 64), f32(0))
    consts[:, C_O96:C_O96 + P] = 1 / DV
    consts[:, C_MASK:C_MASK + P] = np.where(same & (idx[:, None] <= idx[None, :]), f32(1), f32(0))
    consts[:, C_START:C_START + SEQ] = np.where(np.arange(SEQ) % CHUNK == 0, f32(0), f32(1))
    consts[:, C_AVG] = 1 / D

    def features(t):
        return np.ascontiguousarray(t.T.reshape(KT, P, t.shape[0]).transpose(1, 0, 2))

    arrays = {
        "x_in": features(a["x"][0]), "mem_in": features(a["mem"][0]), "consts_in": consts,
        "vecs_in": vecs, "mats_in": mats,
        "w_in1": ffn_in(a["ffn1_w_in"]), "w_out1": ffn_out(a["ffn1_w_out"]),
        "w_in2": ffn_in(a["ffn2_w_in"]), "w_out2": ffn_out(a["ffn2_w_out"]),
        "w_mix": w_mix, "w_v": w_v, "w_mixout": tiles(mo, MIXK), "w_kv": w_kv,
        "w_q": tiles(a["xa_w_q"]), "w_o": tiles(a["xa_w_o"]),
    }
    nc = bacc.Bacc("TRN2", target_bir_lowering=False, num_devices=1)
    args = [nc.dram_tensor(n, t.shape, mybir.dt.from_np(t.dtype), kind="ExternalInput").ap()
            for n, t in arrays.items()]
    out = nc.dram_tensor("out", (P, KT, SEQ), F32, kind="ExternalOutput").ap()
    hybrid_decoder(nc, *args, out)
    r = run(nc, [arrays], core_ids=[0])
    got = r.results[0]["out"]
    return np.ascontiguousarray(got.transpose(1, 0, 2).reshape(D, SEQ).T)[None]
```
